# Optimizing a Trainium2 kernel written in Bass

```python
import jax, jax.numpy as jnp
from jax import lax
import numpy as np

D_MODEL = 1024
BATCH = 1
SEQ = 512
DEPTH = 1

CHUNK = 64
MIX_WIDTH = D_MODEL
GMLP_WIDTH = MIX_WIDTH // 2
GMLP_GROUPS = 4
GMLP_GROUP_CH = GMLP_WIDTH // GMLP_GROUPS
GMLP_BLOCK = 128
FOX_WIDTH = MIX_WIDTH - GMLP_WIDTH
FOX_HEAD_DIM = 64
FOX_HEADS = FOX_WIDTH // FOX_HEAD_DIM
FOX_Q_BLOCK = 128
IN_COLS = 2 * GMLP_WIDTH + 3 * FOX_WIDTH + FOX_HEADS
PLE_DIM = 256
N_EXPERTS = 32
TOP_K = 4
D_EXPERT = D_MODEL
SWIGLU_LIMIT = 7.0
SWIGLU_ALPHA = 1.702
EXPERT_ROWS = 256
RMS_EPS = 1e-5
LN_EPS = 1e-5

kernel_name = "hybrid_gmlp_fox_moe_streaming_encoder"

def rms_norm(x, g):
    xf = x.astype(jnp.float32)
    y = xf * lax.rsqrt(jnp.mean(xf * xf, axis=-1, keepdims=True) + RMS_EPS)
    return (y * g.astype(jnp.float32)).astype(x.dtype)

def layer_norm(x, g, b):
    xf = x.astype(jnp.float32)
    mu = jnp.mean(xf, axis=-1, keepdims=True)
    var = jnp.mean(jnp.square(xf - mu), axis=-1, keepdims=True)
    y = (xf - mu) * lax.rsqrt(var + LN_EPS)
    return (y * g.astype(jnp.float32) + b.astype(jnp.float32)).astype(x.dtype)

def spatial_gating(z_a, ln_g, ln_b, w_s, b_s):
    B, S, _ = z_a.shape
    z = jax.nn.gelu(z_a, approximate=False)
    u, v = jnp.split(z, 2, axis=-1)
    v = layer_norm(v, ln_g, ln_b)
    v = v.reshape(B, S // GMLP_BLOCK, GMLP_BLOCK, GMLP_GROUPS, GMLP_GROUP_CH)
    pos = jnp.arange(GMLP_BLOCK)
    allowed = (pos[None, :] // CHUNK) <= (pos[:, None] // CHUNK)
    ws = jnp.where(allowed[None], w_s, jnp.zeros_like(w_s))
    sv = jnp.einsum('gij,bnjgc->bnigc', ws, v) + b_s.T[None, None, :, :, None]
    return u * sv.reshape(B, S, GMLP_WIDTH)

def forgetting_attention(q, k, v, f_logit, b_f):
    B, S, _ = q.shape
    def heads(t):
        return t.reshape(B, S, FOX_HEADS, FOX_HEAD_DIM).transpose(0, 2, 1, 3)
    q, k, v = heads(q), heads(k), heads(v)
    log_f = jax.nn.log_sigmoid((f_logit + b_f).astype(jnp.float32))
    c = jnp.cumsum(log_f, axis=1).transpose(0, 2, 1)
    scale = FOX_HEAD_DIM ** -0.5
    neg = jnp.finfo(jnp.float32).min
    outs = []
    for qb in range(S // FOX_Q_BLOCK):
        s0 = qb * FOX_Q_BLOCK
        end = s0 + FOX_Q_BLOCK
        logits = jnp.einsum('bhqd,bhkd->bhqk', q[:, :, s0:end], k[:, :, :end]).astype(jnp.float32) * scale
        logits = logits + c[:, :, s0:end, None] - c[:, :, None, :end]
        causal = jnp.arange(end)[None, :] <= (s0 + jnp.arange(FOX_Q_BLOCK))[:, None]
        logits = jnp.where(causal, logits, neg)
        w = jax.nn.softmax(logits, axis=-1).astype(v.dtype)
        outs.append(jnp.einsum('bhqk,bhkd->bhqd', w, v[:, :, :end]))
    o = jnp.concatenate(outs, axis=2)
    return o.transpose(0, 2, 1, 3).reshape(B, S, FOX_WIDTH)

def moe_ffn(xn, w_router, b_router, w_gu, b_gu, w_dn, b_dn):
    B, S, D = xn.shape
    T = B * S
    xt = xn.reshape(T, D)
    logits = (xt @ w_router + b_router).astype(jnp.float32)
    top_v, top_i = lax.top_k(logits, TOP_K)
    gates = jax.nn.softmax(top_v, axis=-1)
    A = T * TOP_K
    flat_e = top_i.reshape(A).astype(jnp.int32)
    flat_tok = jnp.arange(A, dtype=jnp.int32) // TOP_K
    order = jnp.argsort(flat_e, stable=True)
    sorted_e = flat_e[order]
    counts = jnp.bincount(flat_e, length=N_EXPERTS).astype(jnp.int32)
    starts = jnp.cumsum(counts) - counts
    padded = (counts + EXPERT_ROWS - 1) // EXPERT_ROWS * EXPERT_ROWS
    pad_ends = jnp.cumsum(padded)
    pad_starts = pad_ends - padded
    rank = jnp.arange(A, dtype=jnp.int32) - starts[sorted_e]
    dest_sorted = pad_starts[sorted_e] + rank
    n_blocks = -(-A // EXPERT_ROWS) + N_EXPERTS
    P = n_blocks * EXPERT_ROWS
    row_tok = jnp.full((P,), T, dtype=jnp.int32).at[dest_sorted].set(flat_tok[order])
    x_pad = jnp.concatenate([xt, jnp.zeros((1, D), xt.dtype)], axis=0)
    xs = x_pad[row_tok].reshape(n_blocks, EXPERT_ROWS, D)
    block_start = jnp.arange(n_blocks, dtype=jnp.int32) * EXPERT_ROWS
    block_e = jnp.minimum(jnp.searchsorted(pad_ends, block_start, side='right'), N_EXPERTS - 1).astype(jnp.int32)

    def expert_block(args):
        xb, e = args
        h = xb @ w_gu[e] + b_gu[e]
        g, lin = jnp.split(h, 2, axis=-1)
        g = jnp.minimum(g, SWIGLU_LIMIT)
        lin = jnp.clip(lin, -SWIGLU_LIMIT, SWIGLU_LIMIT)
        act = g * jax.nn.sigmoid(SWIGLU_ALPHA * g) * (lin + 1.0)
        return act @ w_dn[e] + b_dn[e]

    ys = lax.map(expert_block, (xs, block_e)).reshape(P, D)
    dest = jnp.zeros((A,), jnp.int32).at[order].set(dest_sorted)
    y = jnp.sum(ys[dest].reshape(T, TOP_K, D) * gates[..., None].astype(ys.dtype), axis=1)
    return y.reshape(B, S, D)

def setup_inputs(seed: int = 0) -> dict:
    key = jax.random.key(seed)
    ks = jax.random.split(key, 24)
    f32 = jnp.float32
    def nrm(k, shape, scale):
        return jax.random.normal(k, shape, f32) * scale
    L, D, E, F = DEPTH, D_MODEL, N_EXPERTS, D_EXPERT
    return {
        "x": nrm(ks[0], (BATCH, SEQ, D), 1.0),
        "p": nrm(ks[1], (DEPTH, BATCH, SEQ, PLE_DIM), 1.0),
        "g_mix": 1.0 + nrm(ks[2], (L, D), 0.05),
        "w_in": nrm(ks[3], (L, D, IN_COLS), D ** -0.5),
        "ln_g": 1.0 + nrm(ks[4], (L, GMLP_WIDTH), 0.05),
        "ln_b": nrm(ks[5], (L, GMLP_WIDTH), 0.02),
        "w_s": nrm(ks[6], (L, GMLP_GROUPS, GMLP_BLOCK, GMLP_BLOCK), GMLP_BLOCK ** -0.5),
        "b_s": 1.0 + nrm(ks[7], (L, GMLP_GROUPS, GMLP_BLOCK), 0.1),
        "b_f": 4.0 + nrm(ks[8], (L, FOX_HEADS), 0.5),
        "g_a": 1.0 + nrm(ks[9], (L, GMLP_WIDTH), 0.05),
        "g_b": 1.0 + nrm(ks[10], (L, FOX_WIDTH), 0.05),
        "w_out": nrm(ks[11], (L, MIX_WIDTH, D), MIX_WIDTH ** -0.5),
        "g_moe": 1.0 + nrm(ks[12], (L, D), 0.05),
        "w_router": nrm(ks[13], (L, D, E), D ** -0.5),
        "b_router": nrm(ks[14], (L, E), 0.01),
        "w_gu": nrm(ks[15], (L, E, D, 2 * F), D ** -0.5),
        "b_gu": nrm(ks[16], (L, E, 2 * F), 0.02),
        "w_dn": nrm(ks[17], (L, E, F, D), F ** -0.5),
        "b_dn": nrm(ks[18], (L, E, D), 0.02),
        "g_ple": 1.0 + nrm(ks[19], (L, D), 0.05),
        "w_ple_gate": nrm(ks[20], (L, D, D), D ** -0.5),
        "w_ple": nrm(ks[21], (L, PLE_DIM, D), PLE_DIM ** -0.5),
        "g_final": 1.0 + nrm(ks[22], (D,), 0.05),
    }

def reference(x, p, g_mix, w_in, ln_g, ln_b, w_s, b_s, b_f, g_a, g_b, w_out,
              g_moe, w_router, b_router, w_gu, b_gu, w_dn, b_dn,
              g_ple, w_ple_gate, w_ple, g_final):
    h = x
    c1 = 2 * GMLP_WIDTH
    c2 = c1 + FOX_WIDTH
    c3 = c2 + FOX_WIDTH
    c4 = c3 + FOX_WIDTH
    for i in range(DEPTH):
        xn = rms_norm(h, g_mix[i])
        z = xn @ w_in[i]
        y_a = spatial_gating(z[..., :c1], ln_g[i], ln_b[i], w_s[i], b_s[i])
        y_b = forgetting_attention(z[..., c1:c2], z[..., c2:c3], z[..., c3:c4], z[..., c4:], b_f[i])
        y = jnp.concatenate([rms_norm(y_a, g_a[i]), rms_norm(y_b, g_b[i])], axis=-1) @ w_out[i]
        h = h + y
        h = h + moe_ffn(rms_norm(h, g_moe[i]), w_router[i], b_router[i], w_gu[i], b_gu[i], w_dn[i], b_dn[i])
        gate = jax.nn.sigmoid(rms_norm(h, g_ple[i]) @ w_ple_gate[i])
        h = h + gate * (p[i] @ w_ple[i])
    return rms_norm(h, g_final)


_drawn_inputs = setup_inputs


def setup_inputs(seed=0):
    import zlib

    import numpy as np

    out = dict(_drawn_inputs(seed))
    spreads = {}
    factors = {'b_gu': 7.247, 'b_dn': 8.0, 'g_ple': 8.0}
    for name, (base, spread) in spreads.items():
        noise = np.random.default_rng([zlib.crc32(name.encode()), seed]).standard_normal(out[name].shape)
        drawn = base * np.exp(spread * noise) if base else spread * noise
        out[name] = __import__('jax').numpy.asarray(drawn.astype(out[name].dtype))
    for name, factor in factors.items():
        out[name] = (out[name] * factor).astype(out[name].dtype)
    return out
```

```python
import concourse.bass as bass
from concourse import mybir
from contextlib import ExitStack

P = 128
SEQ, D = 512, 1024
NT, KD = SEQ // P, D // P
GW, FW, PLE = 512, 512, 256
NH, HD = 8, 64
NG = 4
E, TOPK, F = 32, 4, 1024
ROW = D + E
EXTRA = 15
BANK = 512
NCHUNK = 12
RMS_EPS, LN_EPS = 1e-5, 1e-5
LIMIT, ALPHA = 7.0, 1.702
F32_MIN = -3.4028234663852886e38
OOB = 4096
WIDTHS = (64, 96)


def build(nc, x, p, g_mix, w_in, ln_g, ln_b, w_s, b_s, b_f, g_a, g_b, w_out, g_moe, w_router,
          b_router, w_gu, b_gu, w_dn, b_dn, g_ple, w_ple_gate, w_ple, g_final, out):
    fp32, i32, u32 = mybir.dt.float32, mybir.dt.int32, mybir.dt.uint32
    ALU = mybir.AluOpType
    ACT = mybir.ActivationFunctionType
    AX = mybir.AxisListType.X

    token_rows = nc.dram_tensor("token_rows", [SEQ, ROW], fp32).ap()
    expert_rows = nc.dram_tensor("expert_rows", [SEQ * TOPK, D], fp32).ap()

    x_v = x[0].rearrange("(j p) d -> p j d", p=P)
    out_v = out[0].rearrange("(j p) d -> p j d", p=P)
    p_v = p[0, 0].rearrange("(j p) d -> p j d", p=P)
    win_v = w_in[0].rearrange("(k p) n -> p k n", p=P)
    wout_v = w_out[0].rearrange("(k p) n -> p k n", p=P)
    wpg_v = w_ple_gate[0].rearrange("(k p) n -> p k n", p=P)
    wple_v = w_ple[0].rearrange("(k p) n -> p k n", p=P)
    rows_v = token_rows.rearrange("(j p) d -> p j d", p=P)
    picked_v = expert_rows.rearrange("(j p k) d -> p j k d", p=P, k=TOPK)

    ctx = ExitStack()
    with ctx:
        def sb(name, shape, dt=fp32):
            return ctx.enter_context(nc.sbuf_tensor(name, shape, dt))

        def sem(name):
            return ctx.enter_context(nc.semaphore(name))

        ring = sb("ring", [P, NCHUNK, 2048])
        h = sb("h", [P, NT, D])
        XT = sb("XT", [P, KD, SEQ])
        YC = sb("YC", [P, NT, D])
        VV = sb("VV", [P, 2, NT, 512])
        XS = sb("XS", [P, 2, D])
        QK = sb("QK", [P, 2, 2, 512])
        scr = sb("scr", [P, 4096])
        VA, VT = VV[:, 0], VV[:, 1]
        L = scr[:, 0:1024].rearrange("p (b n) -> p b n", b=2)
        Pr = scr[:, 1024:2048].rearrange("p (b n) -> p b n", b=2)
        PT = scr[:, 2048:3072].rearrange("p (b n) -> p b n", b=2)
        Cb = scr[:, 3072:4096].rearrange("p (b n) -> p b n", b=2)
        bias_nat = scr[0:E, 0:3 * F]
        vec_nat = scr[0:36, 3072:3200]
        ws_nat = YC[:, 0, 512:1024].rearrange("p (g j) -> p g j", g=NG)
        lng, lnb = YC[:, 1, 512:1024], YC[:, 2, 512:1024]
        ident = sb("ident", [P, P])
        TU = sb("TU", [P, SEQ])
        tri, ones = TU[:, 0:P], TU[:, P:2 * P]
        slot1 = sb("slot1", [P, P])
        bT = sb("bT", [P, E, 24])
        vecT = sb("vecT", [P, 36])
        wsT = sb("wsT", [P, NG, P])
        wr = sb("wr", [P, KD, E])
        wf = VV[:, 1, 0, 0:KD * NH].rearrange("p (k n) -> p k n", k=KD)
        bfb = sb("bfb", [P, NH])
        brb = sb("brb", [P, E])
        mhalf = sb("mhalf", [P, NT])
        ss = sb("ss", [P, 7, NT])
        ms = sb("ms", [P, 7, NT])
        rstd = sb("rstd", [P, 7, NT])
        lnst = sb("lnst", [P, NT, 6])
        lnmv = sb("lnmv", [P, NT, 2])
        fl = sb("fl", [P, NT, NH])
        fabs = sb("fabs", [P, NT, NH])
        fln = sb("fln", [P, NT, NH])
        logf = sb("logf", [P, NT, NH])
        ctok = sb("ctok", [P, NT, NH])
        nmax = sb("nmax", [P, 32])
        psumr = sb("psumr", [P, 32])
        rsum = sb("rsum", [P, 32])
        lg = sb("lg", [P, NT, E])
        top = sb("top", [P, NT, 8])
        topi = sb("topi", [P, NT, 8], u32)
        topf = sb("topf", [P, NT, 8])
        gate4 = sb("gate4", [P, NT, TOPK])
        gsum = sb("gsum", [P, NT])
        eid = sb("eid", [P, E])
        kid = sb("kid", [P, TOPK])
        eq = Pr[:, 0, :].rearrange("p (k j e) -> p k j e", k=TOPK, j=NT)
        wq = Pr[:, 1, :].rearrange("p (k j e) -> p k j e", k=TOPK, j=NT)
        wq2 = PT[:, 0, :].rearrange("p (k j e) -> p k j e", k=TOPK, j=NT)
        Mk = sb("Mk", [P, NT, E])
        Gk = sb("Gk", [P, NT, E])
        R1 = sb("R1", [P, NT, E])
        dest = sb("dest", [P, NT, E, 2])
        tok0 = sb("tok0", [P, NT])
        tok4 = sb("tok4", [P, NT])
        cntB = sb("cntB", [P, E])
        extT = sb("extT", [E, 3])
        xin = sb("xin", [P, E])
        jt = sb("jt", [P, 16])
        jb = sb("jb", [P, 16])
        ovc = PT[:, 1, :].rearrange("p (j e) -> p j e", e=E)
        ovv = L[:, 0, :].rearrange("p (j e) -> p j e", e=E)
        ovm = sb("ovm", [P, 16])
        base = sb("base", [P, 48])
        itemf = sb("itemf", [P, 48])
        item_e = sb("item_e", [1, 48], i32)
        cnt_i = sb("cnt_i", [1, E], i32)
        nov_i = sb("nov_i", [1, 1], i32)
        xg = scr[:, 0:ROW]
        selm = scr[:, 1536:2048].rearrange("p (j s) -> p j s", j=NT)
        dcur = scr[:, 2048:2056].rearrange("p (j t) -> p j t", j=NT)
        bcur = scr[:, 2064:2088]
        gcur = scr[:, 2088:2089]
        gnext = scr[:, 2089:2090]
        gidx = scr[:, 2090:2091].bitcast(u32)
        snext = scr[:, 2091:2092].bitcast(u32)
        scur = scr[:, 2092:2093].bitcast(u32)
        pnat = VV[:, 0, 2:4, :].rearrange("p a n -> p (a n)").rearrange("p (j d) -> p j d", j=NT)
        pT = scr[:, 3072:4096].rearrange("p (k t) -> p k t", k=2)
        gbuf = XT[:, 0:2, :].rearrange("p a (b s) -> p (a b) s", b=4)
        ubuf = XT[:, 2:4, :].rearrange("p a (b s) -> p (a b) s", b=4)
        sbuf = XT[:, 4:6, :].rearrange("p a (b s) -> p (a b) s", b=4)
        abuf = XT[:, 6:8, :].rearrange("p a (b s) -> p (a b) s", b=4)
        yts = QK[:, 0, :, :].rearrange("p a (b s) -> p (a b) s", b=4)
        ys = QK[:, 1, :, :].rearrange("p a n -> p (a n)")
        xTm = VV[:, 0, 0:2, :].rearrange("p a (b s) -> p (a b) s", b=4)
        wple_sb = VV[:, 1, :, :].rearrange("p a n -> p (a n)").rearrange("p (k n) -> p k n", k=2)
        PW = YC
        wpg_sb = ring[:, 0:4, :].rearrange("p a (b n) -> p (a b) n", b=2)
        gfin = ring[:, 5, 0:D]
        obuf = ring[:, 4, :].rearrange("p (b n) -> p b n", b=2)
        sg = QK[:, 0, :, :]
        junk = QK[:, 1, :, :].rearrange("p a n -> p (a n)")
        pick = [ring[:, 6 + 2 * j:8 + 2 * j, :].rearrange("p a (b n) -> p (a b) n", b=2) for j in range(3)]
        pick.append(VV[:, :, :, :].rearrange("p a j n -> p (a j n)").rearrange("p (k n) -> p k n", k=TOPK))

        PS = ctx.enter_context(nc.psum_tensor("PS", [P, 8 * BANK], fp32))

        def bank(b, n=1):
            return PS[:, b * BANK:(b + n) * BANK]

        PAIR = [bank(0, 2).rearrange("p (k t) -> p k t", k=KD), bank(2, 2).rearrange("p (k t) -> p k t", k=KD)]
        SM6, SM7 = bank(6), bank(7)
        c_ps = SM7[:, 64:96].rearrange("p (j h) -> p j h", j=NT)
        f_ps = SM7[:, 0:32].rearrange("p (j h) -> p j h", j=NT)
        o_ps = SM7[:, 128:192]
        lg_ps = SM6[:, 0:128].rearrange("p (j e) -> p j e", j=NT)
        rank_ps = SM7[:, 0:128].rearrange("p (j e) -> p j e", j=NT)
        cnt_ps = SM7[:, 128:160]
        cntT_ps = SM7[0:E, 160:161]
        xin_ps = SM6[:, 256:288]
        hT_ps = bank(0, 4).rearrange("p (f s) -> p f s", s=P)
        T_ps = bank(4, 2).rearrange("p (k s) -> p k s", s=P)
        idx_ps = bank(4)[:, 0:2]
        yT_ps = bank(6, 2).rearrange("p (k s) -> p k s", s=P)

        V_MIX, V_A, V_B, V_MOE, V_PLE, V_BS = 0, 8, 12, 16, 24, 32
        def block_at(s):
            return ring[:, s:s + 2, :].rearrange("p a (b n) -> p (a b) n", b=4)
        W_U, W_VA, W_V, W_Q, W_K, W_OA, W_OB = (block_at(s) for s in (8, 10, 0, 2, 4, 6, 8))

        TAIL = [(5, 0), (5, 1), (5, 2), (6, 0), (5, 3), (6, 1), (6, 2), (6, 3)]
        YH = [(s, j) for j in range(NT) for s in (2, 3)] + [(4, j) for j in range(NT)]
        SQ = [(0, j) for j in range(NT)] + YH + TAIL
        POW = [(s, j) for s in (0, 1) for j in range(NT)] + YH + TAIL
        ROUTE = ("bias max0 max1 max2 max3 arg0 arg1 arg2 arg3 argf shift gsum grcp gates eq mk wgate gk wrank "
                 "qk dest0 dest1 c1 cnt ext1 ext2 ext3 xin cmp ecount val vmax clip base0 vneg base1 "
                 "item_e cnt_i nov_i base").split()

        def step(name):
            return ROUTE.index(name) + 1

        def spread(v, n):
            return v.rearrange("p (m a) -> p m a", a=1).to_broadcast([P, v.shape[1], n])

        def stack(v, n):
            return v.rearrange("p (a m) -> p a m", a=1).to_broadcast([P, n, v.shape[1]])

        names = """consts vec_in bias_in ws_in small_in bc_in ln_in wr_in wf_in
            sq_ready ms_ready rstd_ready xs_ready tp_done tp_evac
            vecT_done vecT_ready wsT_ready bT_done bT_ready pre_tp
            unit_done unit_evac sgu_evac h_ready
            f_done fl_ready fexp_ready fln_ready logf_ready c_done ctok_ready
            ln_stat ln_var ln_rstd ln_step va_ready
            cb_done cb_ready s_done l_ready l_masked max_ready p_ready pt_done pt_even pt_odd pv_done r_ready y_ready
            lg_done lg_ready route_step gexp_ready gate_stored rank_done cnt_done ext_ready xin_done tables_ready
            p_in pT_done pT_ready pw_done pw_evac wple_in
            sel_ready idxmm_done gidx_ready xtrans_done xt_ready g_ready u_ready a_ready act_ready
            sig_ready yts_ready ytrans_done ys_ready gate_cur_ready sidx_cur_ready gnext_ready bcur_ready
            gathered scattered chunk_used woutb_in
            zero7 sum_step hsum_ready sg_ready ple_step ple_ready out_ready wpg_in gfin_in""".split()
        S = {n: sem(n) for n in names}
        x_in = [sem(f"x_in{j}") for j in range(NT)]
        blk_in = {n: sem(f"blk_{n}") for n in ("u", "va", "v", "q", "k", "oa", "ob")}
        arrived = [sem(f"arrived{c}") for c in range(NCHUNK)]
        xs_stored = [sem(f"xs_stored{j}") for j in range(NT)]
        out_stored = [sem(f"out_stored{j}") for j in range(NT)]
        pick_in = [sem(f"pick_in{j}") for j in range(NT)]

        block = ctx.enter_context(nc.Block())

        N_PROJ, N_SGU = 20, 24

        def chunk_src(e, c):
            if c < 8:
                return w_gu[0, e, c * P:(c + 1) * P, :]
            r = (c - 8) * 2 * P
            return w_dn[0, e, r:r + 2 * P, :].rearrange("(b p) n -> p b n", p=P)

        def chunk_dst(c):
            return ring[:, c, :] if c < 8 else ring[:, c, :].rearrange("p (b n) -> p b n", b=2)

        def row_bc(v):
            return v[0:1, :].to_broadcast([P, v.shape[1]])

        @block.sync
        def _(sp):
            def load_block(name, dst, src):
                sp.dma_start(dst, src).then_inc(blk_in[name], 16)

            for j in range(NT):
                sp.dma_start(h[:, j, :], x_v[:, j, :]).then_inc(x_in[j], 16)
            load_block("u", W_U, win_v[:, :, 0:512])
            load_block("va", W_VA, win_v[:, :, 512:1024])
            load_block("v", W_V, win_v[:, :, 2048:2560])
            load_block("q", W_Q, win_v[:, :, 1024:1536])
            load_block("k", W_K, win_v[:, :, 1536:2048])
            load_block("oa", W_OA, wout_v[:, :, 0:512])
            sp.wait_ge(S["unit_done"], 8)
            load_block("ob", W_OB, wout_v[:, :, 512:1024])
            sp.wait_ge(S["unit_done"], 12)
            for c in (0, 1):
                sp.dma_start(chunk_dst(c), chunk_src(0, c)).then_inc(arrived[c], 16)
            sp.wait_ge(S["unit_done"], N_PROJ)
            for c in (2, 3, 4, 5, 10, 11):
                sp.dma_start(chunk_dst(c), chunk_src(0, c)).then_inc(arrived[c], 16)
            sp.wait_ge(S["unit_done"], N_SGU)
            sp.dma_start(pnat, p_v).then_inc(S["p_in"], 16)
            sp.wait_ge(S["pv_done"], 32)
            sp.dma_start(wple_sb, wple_v).then_inc(S["wple_in"], 16)
            sp.wait_ge(S["unit_done"], 32)
            for c in (6, 7, 8, 9):
                sp.dma_start(chunk_dst(c), chunk_src(0, c)).then_inc(arrived[c], 16)

            def load_item(i, e):
                for c in range(NCHUNK):
                    sp.wait_ge(S["chunk_used"], (i - 1) * NCHUNK + c + 1)
                    sp.dma_start(chunk_dst(c), chunk_src(e, c)).then_inc(arrived[c], 16)

            with sp.Fori(1, E) as i:
                load_item(i, i)
            sp.wait_ge(S["route_step"], step("base"))
            nov = sp.value_load(nov_i[0:1, 0:1], min_val=0, max_val=EXTRA)
            with sp.Fori(0, EXTRA) as j:
                with sp.If(j < nov):
                    e = sp.value_load(item_e[0:1, bass.ds(j + E, 1)], min_val=0, max_val=E - 1)
                    load_item(j + E, e)
            sp.wait_ge(S["chunk_used"], (nov + (E - 1)) * NCHUNK + 8)
            sp.dma_start(wpg_sb, wpg_v).then_inc(S["wpg_in"], 16)
            sp.dma_start(gfin, row_bc(g_final.rearrange("(a n) -> a n", a=1))).then_inc(S["gfin_in"], 16)
            sp.wait_ge(S["chunk_used"], (nov + E) * NCHUNK)
            sp.wait_ge(S["scattered"], (nov + (E + 1)) * 16)
            for j in range(NT):
                sp.dma_start(pick[j], picked_v[:, j, :, :]).then_inc(pick_in[j], 16)
            for j in range(NT):
                sp.wait_ge(S["out_ready"], j + 1)
                sp.dma_start(out_v[:, j, :], obuf[:, j % 2, :]).then_inc(out_stored[j], 16)
            for j in range(NT):
                sp.wait_ge(out_stored[j], 16)

        @block.gpsimd
        def _(pool):
            pool.memset(ident[:, :], 0.0).then_inc(S["consts"], 1)
            pool.memset(TU[:, :], 1.0).then_inc(S["consts"], 1)
            pool.memset(mhalf[:, :], -0.5).then_inc(S["consts"], 1)
            pool.wait_ge(S["consts"], 3)
            pool.affine_select(out=ident[:, :], in_=ident[:, :], compare_op=ALU.not_equal, fill=1.0, base=0,
                               pattern=[[-1, P]], channel_multiplier=1).then_inc(S["consts"], 1)
            pool.affine_select(out=tri, in_=tri, compare_op=ALU.is_ge, fill=0.0, base=0,
                               pattern=[[1, P]], channel_multiplier=-1).then_inc(S["consts"], 1)

            def iota(dst, pattern, base_, cm):
                pool.iota(dst, pattern, base=base_, channel_multiplier=cm,
                          allow_small_or_imprecise_dtypes=True).then_inc(S["consts"], 1)

            iota(slot1[:, :], [[1, P]], 1, 0)
            iota(eid[:, :], [[1, E]], 0, 0)
            iota(kid[:, :], [[1, TOPK]], 0, 0)
            iota(tok0[:, :], [[P, NT]], -SEQ, 1)
            iota(tok4[:, :], [[P * TOPK, NT]], -SEQ * TOPK, TOPK)
            iota(jt[:, :], [[1, 16]], 0, 0)
            iota(jb[:, :], [[P, 16]], P, 0)
            iota(itemf[:, :], [[1, 48]], 0, 0)

            def power(s, j):
                pool.wait_ge(S["ms_ready"], POW.index((s, j)) + 1)
                pool.tensor_tensor(rstd[:, s, j:j + 1], ms[:, s, j:j + 1], mhalf[:, j:j + 1],
                                   ALU.pow).then_inc(S["rstd_ready"], 1)

            for s_, j in POW[:2 * NT]:
                power(s_, j)
            for n in range(32):
                qb = n % NT
                pool.wait_ge(S["l_ready"], n + 1)
                diag = L[:, n % 2, qb * P:(qb + 1) * P]
                pool.affine_select(out=diag, in_=diag, compare_op=ALU.is_ge, fill=F32_MIN, base=0,
                                   pattern=[[-1, P]], channel_multiplier=1).then_inc(S["l_masked"], 1)
            for s_, j in YH:
                power(s_, j)

            bound = pool.alloc_register("bound")
            pool.reg_mov(bound, 0)

            def gather(n):
                pool.wait_ge(S["gidx_ready"], n)
                pool.reg_alu(bound, bound, SEQ - 1, ALU.max)
                pool.reg_alu(bound, bound, SEQ - 1, ALU.min)
                pool.indirect_dma_start(xg, None, token_rows, bass.IndirectOffsetOnAxis(gidx, 0),
                                        bounds_check=bound, oob_is_err=False).then_inc(S["gathered"], 16)

            def scatter(i):
                pool.wait_ge(S["ys_ready"], i + 1)
                pool.wait_ge(S["sidx_cur_ready"], i + 1)
                pool.reg_alu(bound, bound, SEQ * TOPK - 1, ALU.max)
                pool.indirect_dma_start(expert_rows, bass.IndirectOffsetOnAxis(scur, 0), ys, None,
                                        bounds_check=bound, oob_is_err=False).then_inc(S["scattered"], 16)

            for j in range(NT):
                pool.wait_ge(xs_stored[j], 16)
            pool.wait_ge(S["gate_stored"], 16)
            gather(1)

            def item(i):
                scatter(i)
                gather(i + 2)

            with pool.Fori(0, E) as i:
                item(i)
            nov = pool.value_load(nov_i[0:1, 0:1], min_val=0, max_val=EXTRA)
            with pool.Fori(0, EXTRA) as j:
                with pool.If(j < nov):
                    item(j + E)
            scatter(nov + E)
            for s_, j in TAIL:
                power(s_, j)

        @block.scalar
        def _(act):
            def row(v):
                return v.rearrange("(r n) -> r n", n=P)

            for r, v in ((V_MIX, row(g_mix[0])), (V_A, row(g_a[0])), (V_B, row(g_b[0])), (V_MOE, row(g_moe[0])),
                         (V_PLE, row(g_ple[0])), (V_BS, b_s[0])):
                act.dma_start(vec_nat[r:r + v.shape[0], :], v).then_inc(S["vec_in"], 16)
            act.dma_start(bias_nat[:, 0:2 * F], b_gu[0]).then_inc(S["bias_in"], 16)
            act.dma_start(bias_nat[:, 2 * F:3 * F], b_dn[0]).then_inc(S["bias_in"], 16)
            act.dma_start(ws_nat, w_s[0].rearrange("g i j -> i g j")).then_inc(S["ws_in"], 16)
            act.dma_start(wf[:, :, :], win_v[:, :, 2560:2568]).then_inc(S["wf_in"], 16)
            act.dma_start(wr[:, :, :], w_router[0].rearrange("(k p) n -> p k n", p=P)).then_inc(S["wr_in"], 16)
            act.dma_start(bfb[:, :], row_bc(b_f)).then_inc(S["bc_in"], 16)
            act.dma_start(brb[:, :], row_bc(b_router)).then_inc(S["bc_in"], 16)
            act.dma_start(lng, row_bc(ln_g)).then_inc(S["ln_in"], 16)
            act.dma_start(lnb, row_bc(ln_b)).then_inc(S["ln_in"], 16)

            def square(src, s, j, to):
                n = SQ.index((s, j))
                if n >= 2:
                    act.wait_ge(S["sq_ready"], n - 1 if s < 5 else n)
                act.activation(to, src, ACT.Square, accum_out=ss[:, s, j:j + 1]).then_inc(S["sq_ready"], 1)

            for j in range(NT):
                act.wait_ge(x_in[j], 16)
                square(h[:, j, :].rearrange("p (a n) -> p a n", a=2), 0, j,
                       VV[:, 0, 2 * (j % 2):2 * (j % 2) + 2, :])
            act.wait_ge(S["fl_ready"], 2)
            act.activation(fabs[:, :, :], fabs[:, :, :], ACT.Exp).then_inc(S["fexp_ready"], 1)
            act.wait_ge(S["fexp_ready"], 1)
            act.activation(fln[:, :, :], fabs[:, :, :], ACT.Ln, bias=1.0).then_inc(S["fln_ready"], 1)

            def evac(u, dst, func, scale=1.0):
                act.wait_ge(S["unit_done"], u + 1)
                act.activation(dst, bank(4 + u % 2), func, scale=scale).then_inc(S["unit_evac"], 1)

            for j in range(NT):
                evac(2 * j, YC[:, j, 0:512], ACT.Gelu)
                evac(2 * j + 1, VA[:, j, :], ACT.Gelu)
            for j in range(NT):
                evac(8 + j, VT[:, j, :], ACT.Copy)

            def cb_evac(hh):
                act.wait_ge(S["cb_done"], hh + 1)
                if hh >= 2:
                    act.wait_ge(S["l_ready"], 4 * (hh - 1))
                act.activation(Cb[:, hh % 2, :], SM6, ACT.Copy).then_inc(S["cb_ready"], 1)

            def q_evac(pair):
                if pair >= 2:
                    act.wait_ge(S["s_done"], 8 * (pair - 1))
                evac(12 + 2 * pair, QK[:, 0, pair % 2, :], ACT.Copy, scale=HD ** -0.5)

            def softmax_exp(n):
                w = (n % NT + 1) * P
                act.wait_ge(S["max_ready"], n + 1)
                if n >= 2:
                    act.wait_ge(S["pt_done"], n - 1)
                act.activation(Pr[:, n % 2, 0:w], L[:, n % 2, 0:w], ACT.Exp, bias=nmax[:, n:n + 1],
                               accum_out=psumr[:, n:n + 1]).then_inc(S["p_ready"], 1)

            def pt_evac(n):
                w = (n % NT + 1) * P
                act.wait_ge(S["pt_done"], n + 1)
                if n >= 2:
                    act.wait_ge(S["pv_done"], n - 1)
                act.activation(PT[:, n % 2, 0:w], bank(2 + n % 2)[:, 0:w], ACT.Copy).then_inc(S["pt_odd"], 1)

            q_evac(0)
            evac(13, QK[:, 1, 0, :], ACT.Copy)
            cb_evac(0)
            for n in range(33):
                if n % 4 == 1 and n // 4 + 1 < NH:
                    cb_evac(n // 4 + 1)
                if n % 8 == 3 and n < 24:
                    q_evac(n // 8 + 1)
                if n % 8 == 6 and n < 24:
                    evac(15 + 2 * (n // 8), QK[:, 1, (n // 8 + 1) % 2, :], ACT.Copy)
                if n < 32:
                    softmax_exp(n)
                if n >= 1 and (n - 1) % 2:
                    pt_evac(n - 1)
            act.wait_ge(S["sgu_evac"], NG)
            act.wait_ge(S["y_ready"], 32)
            for j in range(NT):
                square(YC[:, j, 0:512], 2, j, L[:, 0, :])
                square(YC[:, j, 512:1024], 3, j, L[:, 1, :])
            for j in range(NT):
                act.wait_ge(S["h_ready"], 2 * j + 2)
                square(h[:, j, :], 4, j, scr[:, 3072:4096] if j % 2 else scr[:, 1024:2048])
                if j >= 1:
                    act.wait_ge(S["xs_ready"], 2 * NT + j)
                    act.dma_start(rows_v[:, j - 1, 0:D], XS[:, (j - 1) % 2, :]).then_inc(xs_stored[j - 1], 16)
            act.wait_ge(S["xs_ready"], 3 * NT)
            act.dma_start(rows_v[:, NT - 1, 0:D], XS[:, (NT - 1) % 2, :]).then_inc(xs_stored[-1], 16)
            act.wait_ge(S["route_step"], step("shift"))
            act.activation(gate4[:, :, :], gate4[:, :, :], ACT.Exp).then_inc(S["gexp_ready"], 1)
            act.wait_ge(S["route_step"], step("gk"))
            act.dma_start(rows_v[:, :, D:ROW], Gk[:, :, :]).then_inc(S["gate_stored"], 16)
            for u in range(8):
                act.wait_ge(S["pw_done"], u + 1)
                act.activation(PW[:, u // 2, (u % 2) * 512:(u % 2) * 512 + 512], bank(u % 2), ACT.Copy)\
                   .then_inc(S["pw_evac"], 1)

            def scale_rows(i):
                act.wait_ge(S["ytrans_done"], i + 1)
                act.wait_ge(S["gate_cur_ready"], i + 1)
                act.wait_ge(S["scattered"], i * 16)
                act.activation(ys[:, 0:512], bank(4), ACT.Copy, scale=gcur)
                act.activation(ys[:, 512:1024], bank(5), ACT.Copy, scale=gcur).then_inc(S["ys_ready"], 1)

            def item(i):
                scale_rows(i)
                for f in range(8):
                    act.wait_ge(S["g_ready"], i * 8 + (f + 1))
                    act.activation(sbuf[:, f, :], gbuf[:, f, :], ACT.Sigmoid, scale=ALPHA).then_inc(S["sig_ready"], 1)
                act.wait_ge(S["chunk_used"], (i + 1) * NCHUNK)
                for d in range(KD):
                    last = act.activation(yts[:, d, :], yT_ps[:, d, :], ACT.Identity,
                                          bias=bcur[:, 16 + d:17 + d])
                last.then_inc(S["yts_ready"], 1)

            with act.Fori(0, E) as i:
                item(i)
            nov = act.value_load(nov_i[0:1, 0:1], min_val=0, max_val=EXTRA)
            with act.Fori(0, EXTRA) as j:
                with act.If(j < nov):
                    item(j + E)
            scale_rows(nov + E)

            def tail_square(s, j):
                if s == 5:
                    act.wait_ge(S["hsum_ready"], j + 1)
                else:
                    act.wait_ge(S["ple_ready"], 2 * j + 2)
                square(h[:, j, :], s, j, junk)

            def gate_sigmoids(j):
                for c in range(2):
                    k = 2 * j + c
                    act.wait_ge(S["unit_done"], 32 + k + 1)
                    if k >= 2:
                        act.wait_ge(S["ple_ready"], k - 1)
                    act.activation(sg[:, c, :], bank(4 + c), ACT.Sigmoid).then_inc(S["sg_ready"], 1)

            for s_, j in TAIL[:2]:
                tail_square(s_, j)
            gate_sigmoids(0)
            tail_square(5, 2)
            tail_square(6, 0)
            gate_sigmoids(1)
            tail_square(5, 3)
            tail_square(6, 1)
            gate_sigmoids(2)
            tail_square(6, 2)
            gate_sigmoids(3)
            tail_square(6, 3)

        @block.tensor
        def _(pe):
            def mm(dst, lhsT, rhs, start, stop, shared=False):
                return pe.matmul(dst, lhsT, rhs, start=start, stop=stop, skip_group_check=shared)

            def transpose_tile(n):
                pe.wait_ge(S["xs_ready"], n + 1)
                if n >= 2:
                    pe.wait_ge(S["tp_evac"], n - 1)
                for k in range(KD):
                    last = pe.transpose(PAIR[n % 2][:, k, :], XS[:, n % 2, k * P:(k + 1) * P], ident[:, :])
                last.then_inc(S["tp_done"], 1)

            pe.wait_ge(S["consts"], 5)
            pe.wait_ge(S["vec_in"], 96)
            pe.transpose(SM6[:, 0:36], vec_nat, ident[0:36, 0:36]).then_inc(S["vecT_done"], 1)
            for j in range(NT):
                transpose_tile(j)
            pe.wait_ge(S["tp_evac"], NT)
            pe.wait_ge(S["bias_in"], 32)
            for t in range(24):
                last = pe.transpose(bank(0, 2)[:, t * E:(t + 1) * E], bias_nat[:, t * P:(t + 1) * P], ident[0:E, 0:E])
            last.then_inc(S["bT_done"], 1)
            pe.wait_ge(S["ws_in"], 16)
            for g in range(NG):
                last = pe.transpose(bank(2)[:, g * P:(g + 1) * P], ws_nat[:, g, :], ident[:, :])
            last.then_inc(S["bT_done"], 1)
            pe.wait_ge(S["wf_in"], 16)
            pe.wait_ge(S["zero7"], 1)
            for j in range(NT):
                for k in range(KD):
                    last = mm(f_ps[:, j, :], XT[:, k, j * P:(j + 1) * P], wf[:, k, :], k == 0, k == KD - 1)
            last.then_inc(S["f_done"], 1)

            def free_unit(u):
                if 2 <= u < N_PROJ + 2:
                    pe.wait_ge(S["unit_evac"], u - 1)
                elif N_PROJ + 2 <= u < N_SGU + 2:
                    pe.wait_ge(S["sgu_evac"], u - N_PROJ - 1)
                elif N_SGU + 2 <= u < 32:
                    pe.wait_ge(S["h_ready"], u - N_SGU - 1)
                elif u >= 34:
                    pe.wait_ge(S["sg_ready"], u - 33)

            def unit(u, lhsT, rhs, nk=KD, ks=None):
                ks = range(nk) if ks is None else ks
                if ks[0] == 0:
                    free_unit(u)
                for k in ks:
                    last = mm(bank(4 + u % 2), lhsT(k), rhs(k), k == 0, k == nk - 1)
                if ks[-1] == nk - 1:
                    last.then_inc(S["unit_done"], 1)

            def tile_of(j):
                return lambda k: XT[:, k, j * P:(j + 1) * P]

            def cols_of(w, c=None):
                return lambda k: w[:, k, :] if c is None else w[:, k, c * P:(c + 1) * P]

            def all_tokens(k):
                return XT[:, k, :]

            pe.wait_ge(blk_in["u"], 16)
            unit(0, tile_of(0), cols_of(W_U))
            pe.wait_ge(blk_in["va"], 16)
            unit(1, tile_of(0), cols_of(W_VA))
            pe.wait_ge(S["logf_ready"], 1)
            for j in range(NT):
                for i in range(j + 1):
                    last = mm(c_ps[:, j, :], tri if i == j else ones, logf[:, i, :], i == 0, i == j)
            last.then_inc(S["c_done"], 1)
            for j in range(1, NT):
                unit(2 * j, tile_of(j), cols_of(W_U))
                unit(2 * j + 1, tile_of(j), cols_of(W_VA))
            pe.wait_ge(blk_in["v"], 16)
            for j in range(NT):
                unit(8 + j, tile_of(j), cols_of(W_V))
            pe.wait_ge(blk_in["q"], 16)
            unit(12, cols_of(W_Q, 0), all_tokens)
            pe.wait_ge(blk_in["k"], 16)
            unit(13, cols_of(W_K, 0), all_tokens)

            def forget_rows(hh):
                if hh:
                    pe.wait_ge(S["cb_ready"], hh)
                for j in range(NT):
                    last = mm(SM6[:, j * P:SEQ], logf[:, j, hh:hh + 1].to_broadcast([P, P]),
                              TU[:, 0:SEQ - j * P], j == 0, j == NT - 1, True)
                last.then_inc(S["cb_done"], 1)

            def scores(n):
                hh, qb = divmod(n, NT)
                pair, r = divmod(hh, 2)
                if n % 8 == 0:
                    pe.wait_ge(S["unit_evac"], 14 + 2 * pair)
                if n >= 2:
                    pe.wait_ge(S["l_ready"], n - 1)
                mm(bank(n % 2)[:, 0:(qb + 1) * P], QK[r * HD:(r + 1) * HD, 0, pair % 2, qb * P:(qb + 1) * P],
                   QK[r * HD:(r + 1) * HD, 1, pair % 2, 0:(qb + 1) * P], True, True).then_inc(S["s_done"], 1)

            def transpose_probs(n):
                pe.wait_ge(S["p_ready"], n + 1)
                if n >= 2:
                    pe.wait_ge(S["pt_odd" if n % 2 else "pt_even"], n // 2)
                for b in range(n % NT + 1):
                    last = pe.transpose(bank(2 + n % 2)[:, b * P:(b + 1) * P], Pr[:, n % 2, b * P:(b + 1) * P],
                                        ident[:, :])
                last.then_inc(S["pt_done"], 1)

            def values(n):
                hh, qb = divmod(n, NT)
                pe.wait_ge(S["pt_odd" if n % 2 else "pt_even"], n // 2 + 1)
                if n:
                    pe.wait_ge(S["y_ready"], n)
                for b in range(qb + 1):
                    last = mm(o_ps, PT[:, n % 2, b * P:(b + 1) * P], VT[:, b, hh * HD:(hh + 1) * HD],
                              b == 0, b == qb)
                last.then_inc(S["pv_done"], 1)

            pe.wait_ge(S["ctok_ready"], 1)
            pe.wait_ge(S["bT_ready"], 3)
            forget_rows(0)
            SHARE = {0: (0, range(0, 3)), 1: (0, range(3, 6)), 2: (0, range(6, 8)),
                     3: (1, range(0, 3)), 4: (1, range(3, 6)), 5: (1, range(6, 8))}
            for n in range(34):
                if n % 4 == 1 and n // 4 + 1 < NH:
                    forget_rows(n // 4 + 1)
                if n < 32:
                    scores(n)
                if n < 24 and n % 8 in SHARE:
                    kind, ks = SHARE[n % 8]
                    pair = n // 8 + 1
                    unit(12 + 2 * pair + kind, cols_of((W_Q, W_K)[kind], pair), all_tokens, ks=ks)
                if 26 <= n < 30:
                    g = n - 26
                    if g == 0:
                        pe.wait_ge(S["va_ready"], NT)
                    unit(N_PROJ + g, lambda k: wsT[:, g, :], lambda k: VA[:, :, g * P:(g + 1) * P], nk=1)
                if 1 <= n <= 32:
                    transpose_probs(n - 1)
                if n >= 2:
                    values(n - 2)

            def out_projection(j):
                pe.wait_ge(S["tp_evac"], NT + j + 1)
                if j == 0:
                    pe.wait_ge(blk_in["oa"], 16)
                    pe.wait_ge(blk_in["ob"], 16)
                unit(N_SGU + 2 * j, tile_of(j), cols_of(W_OA))
                unit(N_SGU + 2 * j + 1, tile_of(j), cols_of(W_OB))

            transpose_tile(4)
            transpose_tile(5)
            out_projection(0)
            transpose_tile(6)
            out_projection(1)
            transpose_tile(7)
            out_projection(2)
            transpose_tile(8)
            out_projection(3)
            transpose_tile(9)
            transpose_tile(10)
            transpose_tile(11)
            pe.wait_ge(S["tp_evac"], 12)
            pe.wait_ge(S["p_in"], 16)
            for k in range(2):
                for j in range(NT):
                    last = pe.transpose(bank(2 + k)[:, j * P:(j + 1) * P], pnat[:, j, k * P:(k + 1) * P], ident[:, :])
            last.then_inc(S["pT_done"], 1)
            pe.wait_ge(S["wr_in"], 16)
            for j in range(NT):
                for k in range(KD):
                    last = mm(lg_ps[:, j, :], XT[:, k, j * P:(j + 1) * P], wr[:, k, :], k == 0, k == KD - 1)
            last.then_inc(S["lg_done"], 1)
            pe.wait_ge(S["pT_ready"], 1)
            pe.wait_ge(S["wple_in"], 16)

            def ple_product(u):
                j, c = divmod(u, 2)
                if u >= 2:
                    pe.wait_ge(S["pw_evac"], u - 1)
                for k in range(2):
                    last = mm(bank(u % 2), pT[:, k, j * P:(j + 1) * P], wple_sb[:, k, c * 512:(c + 1) * 512],
                              k == 0, k == 1)
                last.then_inc(S["pw_done"], 1)

            for u in range(4):
                ple_product(u)
            pe.wait_ge(S["route_step"], step("mk"))
            for j in range(NT):
                for i in range(j + 1):
                    mm(rank_ps[:, j, :], tri if i == j else ones, Mk[:, i, :], i == 0, i == j)
            for j in range(NT):
                mm(cnt_ps, ones, Mk[:, j, :], j == 0, j == NT - 1)
            for j in range(NT):
                last = mm(cntT_ps, Mk[:, j, :], ones[:, 0:1], j == 0, j == NT - 1)
            last.then_inc(S["rank_done"], 1)
            for u in range(4, 6):
                ple_product(u)
            pe.wait_ge(S["route_step"], step("ext3"))
            mm(xin_ps, extT[:, 2:3].to_broadcast([E, P]), TU[0:E, 0:E], True, True).then_inc(S["xin_done"], 1)
            for u in range(6, 8):
                ple_product(u)

            def list_tokens(n):
                pe.wait_ge(S["sel_ready"], n)
                for j in range(NT):
                    last = mm(idx_ps, selm[:, j, :], dcur[:, j, :], j == 0, j == NT - 1)
                last.then_inc(S["idxmm_done"], 1)

            def transpose_rows(n):
                pe.wait_ge(S["gathered"], n * 16)
                pe.wait_ge(S["gidx_ready"], n)
                for k in range(KD):
                    last = pe.transpose(T_ps[:, k, :], xg[:, k * P:(k + 1) * P], ident[:, :])
                last.then_inc(S["xtrans_done"], 1)

            def transpose_out(i):
                pe.wait_ge(S["yts_ready"], i + 1)
                for k in range(KD):
                    last = pe.transpose(T_ps[:, k, :], yts[:, k, :], ident[:, :])
                last.then_inc(S["ytrans_done"], 1)

            def item(i, w):
                pe.wait_ge(S["xt_ready"], i + 1)
                for k in range(KD):
                    pe.wait_ge(arrived[k], (i + 1) * 16)
                    for f in range(16):
                        last = mm(hT_ps[:, f, 0:w], ring[:, k, f * P:(f + 1) * P], xTm[:, k, 0:w],
                                  k == 0 and f % 4 == 0, k == KD - 1, True)
                    last.then_inc(S["chunk_used"], 1)
                    if k == 1:
                        transpose_out(i)
                    if k == 3:
                        pe.wait_ge(S["ys_ready"], i + 1)
                        list_tokens(i + 2)
                transpose_rows(i + 2)
                pe.wait_ge(S["yts_ready"], i + 1)
                for f in range(8):
                    if f % 2 == 0:
                        pe.wait_ge(arrived[8 + f // 2], (i + 1) * 16)
                    pe.wait_ge(S["act_ready"], i * 8 + (f + 1))
                    for d in range(KD):
                        lo = (f % 2) * D + d * P
                        last = mm(yT_ps[:, d, 0:w], ring[:, 8 + f // 2, lo:lo + P], abuf[:, f, 0:w],
                                  f == 0 and d % 4 == 0, f == 7, True)
                    if f % 2:
                        last.then_inc(S["chunk_used"], 1)

            pe.wait_ge(S["pw_evac"], 8)
            pe.wait_ge(S["route_step"], step("base"))
            list_tokens(1)
            transpose_rows(1)
            with pe.Fori(0, E) as i:
                cnt = pe.value_load(cnt_i[0:1, bass.ds(i, 1)], min_val=0, max_val=SEQ)
                with pe.If(cnt <= WIDTHS[0]):
                    item(i, WIDTHS[0])
                with pe.Else():
                    with pe.If(cnt <= WIDTHS[1]):
                        item(i, WIDTHS[1])
                    with pe.Else():
                        item(i, P)
            nov = pe.value_load(nov_i[0:1, 0:1], min_val=0, max_val=EXTRA)
            with pe.Fori(0, EXTRA) as j:
                with pe.If(j < nov):
                    item(j + E, P)
            pe.wait_ge(S["xt_ready"], nov + (E + 1))
            transpose_out(nov + E)
            pe.wait_ge(S["wpg_in"], 16)
            for j in range(NT):
                transpose_tile(12 + j)
                pe.wait_ge(S["tp_evac"], 12 + j + 1)
                for c in range(2):
                    unit(32 + 2 * j + c, tile_of(j), lambda k: wpg_sb[:, k, c * 512:(c + 1) * 512])

        @block.vector
        def _(dve):
            ts, tt, stt = dve.tensor_scalar, dve.tensor_tensor, dve.scalar_tensor_tensor

            def mean_square(s, j, n):
                dve.wait_ge(S["sq_ready"], SQ.index((s, j)) + 1)
                ts(ms[:, s, j:j + 1], ss[:, s, j:j + 1], 1.0 / n, RMS_EPS, ALU.mult, ALU.add)\
                    .then_inc(S["ms_ready"], 1)

            def rstd_of(s, j):
                dve.wait_ge(S["rstd_ready"], POW.index((s, j)) + 1)
                return rstd[:, s, j:j + 1]

            def normalise(n, pieces):
                scales = [(lo, src, rstd_of(s, j)) for lo, src, s, j in pieces]
                if n >= 2:
                    dve.wait_ge(S["tp_done"], n - 1)
                if n in (10, 11):
                    dve.wait_ge(xs_stored[n - 10], 16)
                for lo, src, r in scales:
                    last = ts(XS[:, n % 2, lo:lo + src.shape[1]], src, r, None, ALU.mult)
                last.then_inc(S["xs_ready"], 1)

            def take_transposed(n, v):
                j = n % NT
                dve.wait_ge(S["tp_done"], n + 1)
                tt(XT[:, :, j * P:(j + 1) * P], PAIR[n % 2], spread(vecT[:, v:v + KD], P),
                   ALU.mult).then_inc(S["tp_evac"], 1)

            dve.memset(SM7, 0.0).then_inc(S["zero7"], 1)
            dve.wait_ge(S["vecT_done"], 1)
            dve.tensor_copy(vecT[:, :], SM6[:, 0:36]).then_inc(S["vecT_ready"], 1)
            dve.wait_ge(S["vecT_ready"], 1)

            def x_scale(j):
                mean_square(0, j, D)
                normalise(j, [(0, h[:, j, :], 0, j)])

            x_scale(0)
            x_scale(1)
            for j in range(NT):
                take_transposed(j, V_MIX)
                if j + 2 < NT:
                    x_scale(j + 2)
            dve.wait_ge(S["bT_done"], 1)
            dve.tensor_copy(bT[:, :, :].rearrange("p e c -> p c e"),
                            bank(0, 2)[:, 0:24 * E].rearrange("p (c e) -> p c e", e=E)).then_inc(S["bT_ready"], 1)
            dve.wait_ge(S["bT_done"], 2)
            dve.tensor_copy(wsT[:, :, :], bank(2).rearrange("p (g i) -> p g i", g=NG)).then_inc(S["bT_ready"], 1)
            dve.wait_ge(S["bT_ready"], 2)
            ts(bT[:, :, 8:16], bT[:, :, 8:16], 1.0, None, ALU.add).then_inc(S["bT_ready"], 1)
            dve.memset(wsT[64:P, :, 0:64], 0.0).then_inc(S["wsT_ready"], 1)
            dve.wait_ge(S["f_done"], 1)
            dve.wait_ge(S["bc_in"], 32)
            tt(fl[:, :, :], f_ps, stack(bfb[:, :], NT), ALU.add)\
                .then_inc(S["fl_ready"], 1)
            dve.wait_ge(S["fl_ready"], 1)
            stt(fabs[:, :, :], fl[:, :, :], -1.0, fl[:, :, :], ALU.mult, ALU.min).then_inc(S["fl_ready"], 1)
            dve.wait_ge(S["fln_ready"], 1)
            stt(logf[:, :, :], fl[:, :, :], 0.0, fln[:, :, :], ALU.min, ALU.subtract).then_inc(S["logf_ready"], 1)
            dve.wait_ge(S["c_done"], 1)
            dve.tensor_copy(ctok[:, :, :], c_ps).then_inc(S["ctok_ready"], 1)
            dve.wait_ge(S["ln_in"], 32)
            n_ln = 0
            for j in range(NT):
                dve.wait_ge(S["unit_evac"], 2 * j + 2)
                dve.bn_stats(lnst[:, j, :], VA[:, j, :]).then_inc(S["ln_stat"], 1)
                dve.wait_ge(S["ln_stat"], j + 1)
                dve.bn_aggr(lnmv[:, j, :], lnst[:, j, :]).then_inc(S["ln_var"], 1)
                dve.wait_ge(S["ln_var"], j + 1)
                ts(ms[:, 1, j:j + 1], lnmv[:, j, 1:2], LN_EPS, None, ALU.add).then_inc(S["ms_ready"], 1)
                r = rstd_of(1, j)
                ts(VA[:, j, :], VA[:, j, :], lnmv[:, j, 0:1], r, ALU.subtract, ALU.mult).then_inc(S["ln_step"], 1)
                dve.wait_ge(S["ln_step"], 2 * j + 1)
                tt(VA[:, j, :], VA[:, j, :], lng, ALU.mult).then_inc(S["ln_step"], 1)
                dve.wait_ge(S["ln_step"], 2 * j + 2)
                tt(VA[:, j, :], VA[:, j, :], lnb, ALU.add).then_inc(S["va_ready"], 1)

            def logits(n):
                hh, qb = divmod(n, NT)
                w = (qb + 1) * P
                dve.wait_ge(S["s_done"], n + 1)
                dve.wait_ge(S["cb_ready"], hh + 1)
                if n >= 2:
                    dve.wait_ge(S["p_ready"], n - 1)
                stt(L[:, n % 2, 0:w], bank(n % 2)[:, 0:w], ctok[:, qb, hh:hh + 1], Cb[:, hh % 2, 0:w],
                    ALU.add, ALU.subtract).then_inc(S["l_ready"], 1)

            def row_max(n):
                dve.wait_ge(S["l_masked"], n + 1)
                dve.tensor_reduce(nmax[:, n:n + 1], L[:, n % 2, 0:(n % NT + 1) * P], AX, ALU.max, negate=True)\
                    .then_inc(S["max_ready"], 1)

            def take_probs(n):
                w = (n % NT + 1) * P
                dve.wait_ge(S["pt_done"], n + 1)
                if n >= 2:
                    dve.wait_ge(S["pv_done"], n - 1)
                dve.tensor_copy(PT[:, n % 2, 0:w], bank(2 + n % 2)[:, 0:w]).then_inc(S["pt_even"], 1)

            def outputs(n):
                hh, qb = divmod(n, NT)
                dve.wait_ge(S["p_ready"], n + 1)
                dve.reciprocal(rsum[:, n:n + 1], psumr[:, n:n + 1]).then_inc(S["r_ready"], 1)
                dve.wait_ge(S["r_ready"], n + 1)
                dve.wait_ge(S["pv_done"], n + 1)
                ts(YC[:, qb, GW + hh * HD:GW + (hh + 1) * HD], o_ps, rsum[:, n:n + 1], None, ALU.mult)\
                    .then_inc(S["y_ready"], 1)

            for n in range(35):
                if n < 32:
                    logits(n)
                if 1 <= n <= 32:
                    row_max(n - 1)
                if 2 <= n < 34 and n % 2 == 0:
                    take_probs(n - 2)
                if n >= 3:
                    outputs(n - 3)
                if 27 <= n < 31:
                    g = n - 27
                    cols = YC[:, :, g * P:(g + 1) * P]
                    dve.wait_ge(S["unit_done"], N_PROJ + g + 1)
                    stt(cols, bank(4 + g % 2).rearrange("p (j c) -> p j c", j=NT), vecT[:, V_BS + g:V_BS + g + 1],
                        cols, ALU.add, ALU.mult).then_inc(S["sgu_evac"], 1)

            def y_scale(j):
                mean_square(2, j, GW)
                mean_square(3, j, FW)
                normalise(4 + j, [(0, YC[:, j, 0:GW], 2, j), (GW, YC[:, j, GW:D], 3, j)])

            def residual(j):
                for c in range(2):
                    u = N_SGU + 2 * j + c
                    dve.wait_ge(S["unit_done"], u + 1)
                    tt(h[:, j, c * 512:(c + 1) * 512], h[:, j, c * 512:(c + 1) * 512], bank(4 + c), ALU.add)\
                        .then_inc(S["h_ready"], 1)

            def h_scale(j):
                mean_square(4, j, D)
                normalise(8 + j, [(0, h[:, j, :], 4, j)])

            y_scale(0)
            y_scale(1)
            take_transposed(4, V_A)
            y_scale(2)
            take_transposed(5, V_A)
            residual(0)
            y_scale(3)
            take_transposed(6, V_A)
            residual(1)
            take_transposed(7, V_A)
            h_scale(0)
            residual(2)
            h_scale(1)
            take_transposed(8, V_MOE)
            residual(3)
            h_scale(2)
            take_transposed(9, V_MOE)
            h_scale(3)
            take_transposed(10, V_MOE)
            take_transposed(11, V_MOE)
            dve.wait_ge(S["pT_done"], 1)
            dve.tensor_copy(pT, bank(2, 2).rearrange("p (k t) -> p k t", k=2)).then_inc(S["pT_ready"], 1)

            def r(name, ins, wait=True):
                ins.then_inc(S["route_step"], 1)
                if wait:
                    dve.wait_ge(S["route_step"], step(name))

            dve.wait_ge(S["lg_done"], 1)
            r("bias", tt(lg[:, :, :], lg_ps, stack(brb[:, :], NT),
                         ALU.add))
            for j in range(NT):
                r(f"max{j}", dve.max(top[:, j, :], lg[:, j, :]))
            for j in range(NT):
                r(f"arg{j}", dve.max_index(topi[:, j, :], top[:, j, :], lg[:, j, :]))
            r("argf", dve.tensor_copy(topf[:, :, :], topi[:, :, :]))
            r("shift", tt(gate4[:, :, :], top[:, :, 0:TOPK], top[:, :, 0:1].to_broadcast([P, NT, TOPK]), ALU.subtract))
            dve.wait_ge(S["gexp_ready"], 1)
            r("gsum", dve.tensor_reduce(gsum[:, :], gate4[:, :, :], AX, ALU.add))
            r("grcp", dve.reciprocal(gsum[:, :], gsum[:, :]))
            r("gates", tt(gate4[:, :, :], gate4[:, :, :],
                          spread(gsum[:, :], TOPK), ALU.mult))
            for k in range(TOPK):
                last = tt(eq[:, k], topf[:, :, k:k + 1].to_broadcast([P, NT, E]),
                          stack(eid[:, :], NT), ALU.is_equal)
            r("eq", last)
            r("mk", dve.tensor_reduce(Mk[:, :, :], eq.rearrange("p k j e -> p j e k"), AX, ALU.add))
            for k in range(TOPK):
                last = tt(wq[:, k], eq[:, k], gate4[:, :, k:k + 1].to_broadcast([P, NT, E]), ALU.mult)
            r("wgate", last)
            r("gk", dve.tensor_reduce(Gk[:, :, :], wq.rearrange("p k j e -> p j e k"), AX, ALU.add))
            for k in range(TOPK):
                last = ts(wq2[:, k], eq[:, k], float(k), None, ALU.mult)
            r("wrank", last)
            r("qk", dve.tensor_reduce(dest[:, :, :, 1], wq2.rearrange("p k j e -> p j e k"), AX, ALU.add))
            r("dest0", tt(dest[:, :, :, 1], dest[:, :, :, 1],
                          spread(tok4[:, :], E), ALU.add))
            r("dest1", dve.tensor_copy(dest[:, :, :, 0],
                                       spread(tok0[:, :], E)))
            dve.wait_ge(S["rank_done"], 1)
            r("c1", tt(R1[:, :, :], rank_ps, Mk[:, :, :], ALU.mult))
            r("cnt", dve.tensor_copy(cntB[:, :], cnt_ps))
            r("ext1", ts(extT[:, 0:1], cntT_ps, float(P), None, ALU.is_gt))
            r("ext2", stt(extT[:, 1:2], cntT_ps, 2.0 * P, extT[:, 0:1], ALU.is_gt, ALU.add))
            r("ext3", stt(extT[:, 2:3], cntT_ps, 3.0 * P, extT[:, 1:2], ALU.is_gt, ALU.add))
            dve.wait_ge(S["xin_done"], 1)
            xrow = stack(xin[:, :], 16)
            r("xin", dve.tensor_copy(xin[:, :], xin_ps))
            r("cmp", tt(ovc, xrow, spread(jt[:, :], E), ALU.is_le))
            r("ecount", dve.tensor_reduce(itemf[:, E:48], ovc, AX, ALU.add))
            r("val", tt(ovv, ovc, xrow, ALU.mult))
            r("vmax", dve.tensor_reduce(ovm[:, :], ovv, AX, ALU.max))
            r("clip", ts(itemf[:, E:48], itemf[:, E:48], float(E - 1), None, ALU.min))
            r("base0", dve.memset(base[:, 0:E], 0.0))
            r("vneg", ts(ovm[:, :], ovm[:, :], -float(P), None, ALU.mult))
            r("base1", tt(base[:, E:48], ovm[:, :], jb[:, :], ALU.add))
            r("item_e", dve.tensor_copy(item_e[:, :], itemf[0:1, :]))
            r("cnt_i", dve.tensor_copy(cnt_i[:, :], cntB[0:1, :]))
            r("nov_i", dve.tensor_copy(nov_i[:, :], xin[0:1, E - 1:E]))
            r("base", dve.memset(xg, 0.0))

            def select(e, i, n):
                for j in range(NT):
                    ts(selm[:, j, :], slot1[:, :], base[:, bass.ds(i, 1)], R1[:, j, bass.ds(e, 1)],
                       ALU.add, ALU.is_equal)
                for j in range(NT):
                    last = dve.tensor_copy(dcur[:, j, :], dest[:, j, bass.ds(e, 1), :].rearrange("p a t -> p (a t)"))
                last.then_inc(S["sel_ready"], 1)

            def take_list(n):
                dve.wait_ge(S["idxmm_done"], n)
                ts(gidx, idx_ps[:, 0:1], float(SEQ), None, ALU.add)
                ts(snext, idx_ps[:, 1:2], float(SEQ * TOPK), None, ALU.add).then_inc(S["gidx_ready"], 1)

            def take_rows(e, n):
                dve.wait_ge(S["gathered"], n * 16)
                dve.tensor_copy(gnext, xg[:, bass.ds(e + D, 1)]).then_inc(S["gnext_ready"], 1)
                dve.wait_ge(S["xtrans_done"], n)
                tt(xTm, T_ps, spread(vecT[:, V_MOE:V_MOE + KD], P), ALU.mult).then_inc(S["xt_ready"], 1)

            def item(i):
                dve.wait_ge(S["ys_ready"], i + 1)
                dve.wait_ge(S["gnext_ready"], i + 1)
                dve.tensor_copy(gcur, gnext).then_inc(S["gate_cur_ready"], 1)
                e = dve.value_load(item_e[0:1, bass.ds(i + 1, 1)], min_val=0, max_val=E - 1)
                select(e, i + 1, i + 2)
                dve.wait_ge(S["scattered"], (i + 1) * 16)
                dve.tensor_copy(scur, snext).then_inc(S["sidx_cur_ready"], 1)
                dve.wait_ge(S["sidx_cur_ready"], i + 2)
                take_list(i + 2)
                dve.wait_ge(S["bcur_ready"], i + 1)
                dve.wait_ge(S["chunk_used"], i * NCHUNK + 8)
                for f in range(10):
                    if f < 8:
                        ts(gbuf[:, f, :], hT_ps[:, f, :], bcur[:, f:f + 1], LIMIT, ALU.add, ALU.min)\
                            .then_inc(S["g_ready"], 1)
                        ts(ubuf[:, f, :], hT_ps[:, 8 + f, :], bcur[:, 8 + f:9 + f], LIMIT + 1.0, ALU.add, ALU.min)\
                            .then_inc(S["u_ready"], 1)
                    if 1 <= f < 9:
                        dve.wait_ge(S["u_ready"], i * 8 + f)
                        stt(ubuf[:, f - 1, :], ubuf[:, f - 1, :], 1.0 - LIMIT, gbuf[:, f - 1, :], ALU.max, ALU.mult)\
                            .then_inc(S["a_ready"], 1)
                    if f >= 2:
                        dve.wait_ge(S["a_ready"], i * 8 + (f - 1))
                        dve.wait_ge(S["sig_ready"], i * 8 + (f - 1))
                        tt(abuf[:, f - 2, :], ubuf[:, f - 2, :], sbuf[:, f - 2, :], ALU.mult)\
                            .then_inc(S["act_ready"], 1)
                take_rows(e, i + 2)
                dve.wait_ge(S["yts_ready"], i + 2)
                dve.tensor_copy(bcur, bT[:, bass.ds(e, 1), :].rearrange("p a c -> p (a c)")).then_inc(S["bcur_ready"], 1)

            dve.memset(yts, 0.0).then_inc(S["yts_ready"], 1)
            dve.memset(scur, OOB).then_inc(S["sidx_cur_ready"], 1)
            dve.tensor_copy(bcur, bT[:, 0, :]).then_inc(S["bcur_ready"], 1)
            dve.memset(gcur, 0.0).then_inc(S["gate_cur_ready"], 1)
            select(0, 0, 1)
            take_list(1)
            take_rows(0, 1)
            with dve.Fori(0, E) as i:
                item(i)
            nov = dve.value_load(nov_i[0:1, 0:1], min_val=0, max_val=EXTRA)
            with dve.Fori(0, EXTRA) as j:
                with dve.If(j < nov):
                    item(j + E)

            def sum_rows(j):
                t = pick[j]
                dve.wait_ge(pick_in[j], 16)
                tt(t[:, 0:2, :], t[:, 0:2, :], t[:, 2:4, :], ALU.add).then_inc(S["sum_step"], 1)
                dve.wait_ge(S["sum_step"], 2 * j + 1)
                tt(t[:, 0, :], t[:, 0, :], t[:, 1, :], ALU.add).then_inc(S["sum_step"], 1)
                dve.wait_ge(S["sum_step"], 2 * j + 2)
                tt(h[:, j, :], h[:, j, :], t[:, 0, :], ALU.add).then_inc(S["hsum_ready"], 1)

            def ple_scale(j):
                normalise(12 + j, [(0, h[:, j, :], 5, j)])
                take_transposed(12 + j, V_PLE)

            def add_ple(j):
                for c in range(2):
                    k, cols = 2 * j + c, slice(c * 512, (c + 1) * 512)
                    dve.wait_ge(S["sg_ready"], k + 1)
                    tt(sg[:, c, :], sg[:, c, :], PW[:, j, cols], ALU.mult).then_inc(S["ple_step"], 1)
                    dve.wait_ge(S["ple_step"], k + 1)
                    tt(h[:, j, cols], h[:, j, cols], sg[:, c, :], ALU.add).then_inc(S["ple_ready"], 1)

            def final(j):
                sc = rstd_of(6, j)
                dve.wait_ge(S["gfin_in"], 16)
                if j >= 2:
                    dve.wait_ge(out_stored[j - 2], 16)
                stt(obuf[:, j % 2, :], h[:, j, :], sc, gfin, ALU.mult, ALU.mult).then_inc(S["out_ready"], 1)

            sum_rows(0)
            mean_square(5, 0, D)
            sum_rows(1)
            mean_square(5, 1, D)
            ple_scale(0)
            sum_rows(2)
            mean_square(5, 2, D)
            ple_scale(1)
            add_ple(0)
            mean_square(6, 0, D)
            sum_rows(3)
            mean_square(5, 3, D)
            ple_scale(2)
            add_ple(1)
            final(0)
            mean_square(6, 1, D)
            ple_scale(3)
            add_ple(2)
            final(1)
            mean_square(6, 2, D)
            add_ple(3)
            final(2)
            mean_square(6, 3, D)
            final(3)


_INS = ["x", "p", "g_mix", "w_in", "ln_g", "ln_b", "w_s", "b_s", "b_f", "g_a", "g_b", "w_out", "g_moe", "w_router",
        "b_router", "w_gu", "b_gu", "w_dn", "b_dn", "g_ple", "w_ple_gate", "w_ple", "g_final"]


def kernel(**inputs):
    import numpy as np
    import concourse.bacc as bacc
    from concourse import mybir as mb
    from concourse.bass_utils import run_bass_kernel_spmd as run

    nc = bacc.Bacc("TRN2", target_bir_lowering=False, num_devices=1)
    arrays, args = {}, []
    for name in _INS:
        a = np.ascontiguousarray(inputs[name])
        arrays[f"in_{name}"] = a
        args.append(nc.dram_tensor(f"in_{name}", a.shape, mb.dt.from_np(a.dtype), kind="ExternalInput").ap())
    o = nc.dram_tensor("out_0", (1, SEQ, D), mb.dt.float32, kind="ExternalOutput").ap()
    build(nc, *args, o)
    r = run(nc, [arrays], core_ids=[0])
    return r.results[0]["out_0"]
```

```python
import concourse.bass as bass
from concourse import mybir
from contextlib import ExitStack

P = 128
SEQ, D = 512, 1024
NT, KD = SEQ // P, D // P
GW, FW, PLE = 512, 512, 256
NH, HD = 8, 64
NG = 4
E, TOPK, F = 32, 4, 1024
EXTRA = 15
BANK = 512
NCHUNK = 12
RMS_EPS, LN_EPS = 1e-5, 1e-5
LIMIT, ALPHA = 7.0, 1.702
F32_MIN = -3.4028234663852886e38
OOB = 16384
HALF = P // 2


def build(nc, x, p, g_mix, w_in, ln_g, ln_b, w_s, b_s, b_f, g_a, g_b, w_out, g_moe, w_router,
          b_router, w_gu, b_gu, w_dn, b_dn, g_ple, w_ple_gate, w_ple, g_final, out):
    fp32, bf16, i32, u32 = mybir.dt.float32, mybir.dt.bfloat16, mybir.dt.int32, mybir.dt.uint32
    ALU = mybir.AluOpType
    ACT = mybir.ActivationFunctionType
    AX = mybir.AxisListType.X

    token_rows = nc.dram_tensor("token_rows", [SEQ, D], fp32).ap()
    expert_rows = nc.dram_tensor("expert_rows", [SEQ * TOPK * 2, D // 2], fp32).ap()

    x_v = x[0].rearrange("(j p) d -> p j d", p=P)
    out_v = out[0].rearrange("(j p) d -> p j d", p=P)
    p_v = p[0, 0].rearrange("(j p) d -> p j d", p=P)
    win_v = w_in[0].rearrange("(k p) n -> p k n", p=P)
    wout_v = w_out[0].rearrange("(k p) n -> p k n", p=P)
    wpg_v = w_ple_gate[0].rearrange("(k p) n -> p k n", p=P)
    wple_v = w_ple[0].rearrange("(k p) n -> p k n", p=P)
    rows_v = token_rows.rearrange("(j p) d -> p j d", p=P)
    picked_v = expert_rows.rearrange("(j p k c) d -> p j k (c d)", p=P, k=TOPK, c=2)

    ctx = ExitStack()
    with ctx:
        def sb(name, shape, dt=fp32):
            return ctx.enter_context(nc.sbuf_tensor(name, shape, dt))

        def sem(name):
            return ctx.enter_context(nc.semaphore(name))

        ring = sb("ring", [P, NCHUNK, 2048])
        h = sb("h", [P, NT, D])
        XT = sb("XT", [P, KD, SEQ])
        YC = sb("YC", [P, NT, D])
        VV = sb("VV", [P, 2, NT, 512])
        XS = sb("XS", [P, 2, D])
        QK = sb("QK", [P, 2, 2, 512])
        scr = sb("scr", [P, 4096])
        VA, VT = VV[:, 0], VV[:, 1]
        L = scr[:, 0:1024].rearrange("p (b n) -> p b n", b=2)
        Pr = scr[:, 1024:2048].rearrange("p (b n) -> p b n", b=2)
        PT = scr[:, 2048:3072].rearrange("p (b n) -> p b n", b=2)
        Cb = scr[:, 3072:4096].rearrange("p (b n) -> p b n", b=2)
        bias_raw = ring[0:3 * E, 10:12, :].rearrange("p a n -> p (a n)")[:, 0:3 * F]
        bias3 = scr[0:3 * E, 2560:4096].bitcast(bf16)
        vec_nat = scr[0:36, 3072:3200]
        ws_nat = YC[:, 0, 512:1024].rearrange("p (g j) -> p g j", g=NG)
        lng, lnb = YC[:, 1, 512:1024], YC[:, 2, 512:1024]
        ident = sb("ident", [P, P])
        TU = sb("TU", [P, SEQ])
        tri, ones = TU[:, 0:P], TU[:, P:2 * P]
        slots = sb("slots", [P, 2, P])
        offs = sb("offs", [P, 2, 3])
        eye3 = sb("eye3", [3 * E, E], bf16)
        esel = sb("esel", [3 * E, P], bf16)
        vecT = sb("vecT", [P, 36])
        wsT = sb("wsT", [P, NG, P])
        wr = sb("wr", [P, KD, E])
        wf = VV[:, 1, 0, 0:KD * NH].rearrange("p (k n) -> p k n", k=KD)
        bfb = sb("bfb", [P, NH])
        brb = sb("brb", [P, E])
        mhalf = sb("mhalf", [P, NT])
        ss = sb("ss", [P, 7, NT])
        ms = sb("ms", [P, 7, NT])
        rstd = sb("rstd", [P, 7, NT])
        lnst = sb("lnst", [P, NT, 6])
        lnmv = sb("lnmv", [P, NT, 2])
        fl = sb("fl", [P, NT, NH])
        fabs = sb("fabs", [P, NT, NH])
        fln = sb("fln", [P, NT, NH])
        logf = sb("logf", [P, NT, NH])
        ctok = sb("ctok", [P, NT, NH])
        nmax = sb("nmax", [P, 32])
        psumr = sb("psumr", [P, 32])
        rsum = sb("rsum", [P, 32])
        lg = sb("lg", [P, NT, E])
        top = sb("top", [P, NT, 8])
        topi = sb("topi", [P, NT, 8], u32)
        topf = sb("topf", [P, NT, 8])
        gate4 = sb("gate4", [P, NT, TOPK])
        gsum = sb("gsum", [P, NT])
        eid = sb("eid", [P, E])
        kid = sb("kid", [P, TOPK])
        eq = Pr[:, 0, :].rearrange("p (k j e) -> p k j e", k=TOPK, j=NT)
        wq = Pr[:, 1, :].rearrange("p (k j e) -> p k j e", k=TOPK, j=NT)
        wq2 = PT[:, 0, :].rearrange("p (k j e) -> p k j e", k=TOPK, j=NT)
        Mk = sb("Mk", [P, NT, E])
        R1 = sb("R1", [P, NT, E])
        dest = sb("dest", [P, NT, E, 3])
        tok0 = sb("tok0", [P, NT])
        tok4 = sb("tok4", [P, NT])
        cntB = sb("cntB", [P, E])
        extT = sb("extT", [E, 3])
        xin = sb("xin", [P, E])
        jt = sb("jt", [P, 16])
        jb = sb("jb", [P, 16])
        ovc = L[:, 1, :].rearrange("p (j e) -> p j e", e=E)
        ovv = L[:, 0, :].rearrange("p (j e) -> p j e", e=E)
        ovm = sb("ovm", [P, 16])
        base = sb("base", [P, 48])
        itemf = sb("itemf", [P, 48])
        item_e = sb("item_e", [1, 48], i32)
        item_s = sb("item_s", [1, 48], i32)
        nov_i = sb("nov_i", [1, 1], i32)
        xg = scr[:, 0:D]
        selm = scr[:, 1536:2048].rearrange("p (j s) -> p j s", j=NT)
        dcur = scr[:, 2048:2060].rearrange("p (j t) -> p j t", j=NT)
        ocur = scr[:, 2064:2067]
        gcur = scr[:, 2088:2089]
        gnext = scr[:, 2089:2090]
        gidx = scr[:, 2090:2091].bitcast(u32)
        snext = scr[:, 2092:2094].bitcast(u32)
        scur = scr[:, 2094:2096].bitcast(u32)
        ahead = scr[:, 2100:2102]
        pnat = VV[:, 0, 2:4, :].rearrange("p a n -> p (a n)").rearrange("p (j d) -> p j d", j=NT)
        pT = QK[:, 0, :, :]
        gbuf, ubuf, sbuf = XT[:, 0:2, :], XT[:, 2:4, :], XT[:, 4:6, :]
        aT = XT[:, 6:8, :].rearrange("p a (b s) -> p (a b) s", b=4)
        ys = QK[:, 1, :, :]
        xTm = VV[:, 0, 0:2, :].rearrange("p a (b s) -> p (a b) s", b=4)
        wple_sb = VV[:, 1, :, :].rearrange("p a n -> p (a n)").rearrange("p (k n) -> p k n", k=2)
        PW = YC
        wpg_sb = ring[:, 0:4, :].rearrange("p a (b n) -> p (a b) n", b=2)
        gfin = ring[:, 5, 0:D]
        obuf = ring[:, 4, :].rearrange("p (b n) -> p b n", b=2)
        sg = QK[:, 0, :, :]
        junk = QK[:, 1, :, :].rearrange("p a n -> p (a n)")
        pick = [ring[:, 6 + 2 * j:8 + 2 * j, :].rearrange("p a (b n) -> p (a b) n", b=2) for j in range(3)]
        pick.append(VV[:, :, :, :].rearrange("p a j n -> p (a j n)").rearrange("p (k n) -> p k n", k=TOPK))

        PS = ctx.enter_context(nc.psum_tensor("PS", [P, 8 * BANK], fp32))

        def bank(b, n=1):
            return PS[:, b * BANK:(b + n) * BANK]

        PAIR = [bank(0, 2).rearrange("p (k t) -> p k t", k=KD), bank(2, 2).rearrange("p (k t) -> p k t", k=KD)]
        SM6, SM7 = bank(6), bank(7)
        c_ps = SM7[:, 64:96].rearrange("p (j h) -> p j h", j=NT)
        f_ps = SM7[:, 0:32].rearrange("p (j h) -> p j h", j=NT)
        o_ps = SM7[:, 128:192]
        lg_ps = SM6[:, 0:128].rearrange("p (j e) -> p j e", j=NT)
        rank_ps = SM7[:, 0:128].rearrange("p (j e) -> p j e", j=NT)
        cnt_ps = SM7[:, 128:160]
        cntT_ps = SM7[0:E, 160:161]
        xin_ps = SM6[:, 256:288]
        T_ps = bank(4, 2).rearrange("p (k s) -> p k s", s=P)
        idx_ps = bank(4)[:, 0:3]

        V_MIX, V_A, V_B, V_MOE, V_PLE, V_BS = 0, 8, 12, 16, 24, 32
        def block_at(s):
            return ring[:, s:s + 2, :].rearrange("p a (b n) -> p (a b) n", b=4)
        W_U, W_VA, W_V, W_Q, W_K, W_OA, W_OB = (block_at(s) for s in (8, 10, 0, 2, 4, 6, 8))

        TAIL = [(5, 0), (5, 1), (5, 2), (6, 0), (5, 3), (6, 1), (6, 2), (6, 3)]
        YH = [(s, j) for j in range(NT) for s in (2, 3)] + [(4, j) for j in range(NT)]
        SQ = [(0, j) for j in range(NT)] + YH + TAIL
        POW = [(s, j) for s in (0, 1) for j in range(NT)] + YH + TAIL
        ROUTE = ("bias max0 max1 max2 max3 arg0 arg1 arg2 arg3 argf shift gsum grcp gates eq mk wgate gk wrank "
                 "qk dest0 dest1 c1 cnt ext1 ext2 ext3 xin cmp ecount val vmax clip base0 vneg base1 "
                 "item_e small0 small1 nov_i base").split()

        def step(name):
            return ROUTE.index(name) + 1

        def spread(v, n):
            return v.rearrange("p (m a) -> p m a", a=1).to_broadcast([P, v.shape[1], n])

        def stack(v, n):
            return v.rearrange("p (a m) -> p a m", a=1).to_broadcast([P, n, v.shape[1]])

        names = """consts vec_in bias_in ws_in bc_in ln_in wr_in wf_in
            sq_ready ms_ready rstd_ready xs_ready tp_done tp_evac
            vecT_done vecT_ready wsT_ready ws_done ws_evac bias_part bias_rest eye_ready
            unit_done unit_evac sgu_evac h_ready
            f_done fl_ready fexp_ready fln_ready logf_ready c_done ctok_ready
            ln_stat ln_var ln_step va_ready
            cb_done cb_ready s_done l_ready l_masked max_ready p_ready pt_done pt_even pt_odd pv_done r_ready y_ready
            lg_done lg_ready route_step gexp_ready rank_done cnt_done ext_ready xin_done
            p_in pT_done pT_ready pw_done pw_evac wple_in
            sel_ready idxmm_done gidx_ready places_ready xtrans_done xt_ready esel_ready offs_ready
            gu_done g_ready u_ready a_ready act_ready sig_ready atrans_done at_ready
            ys_ready cur_ready gathered scattered_a scattered_b chunk_used
            zero7 sum_step hsum_ready sg_ready ple_step ple_ready out_ready wpg_in gfin_in""".split()
        S = {n: sem(n) for n in names}
        x_in = [sem(f"x_in{j}") for j in range(NT)]
        blk_in = {n: sem(f"blk_{n}") for n in ("u", "va", "v", "q", "k", "oa", "ob")}
        arrived = [sem(f"arrived{c}") for c in range(NCHUNK)]
        xs_stored = [sem(f"xs_stored{j}") for j in range(NT)]
        out_stored = [sem(f"out_stored{j}") for j in range(NT)]
        pick_in = [sem(f"pick_in{j}") for j in range(NT)]

        block = ctx.enter_context(nc.Block())

        N_PROJ, N_SGU = 20, 24

        def chunk_src(e, c):
            if c < 8:
                return w_gu[0, e, c * P:(c + 1) * P, :]
            r = (c - 8) * 2 * P
            return w_dn[0, e, r:r + 2 * P, :].rearrange("(b p) n -> p b n", p=P)

        def chunk_dst(c):
            return ring[:, c, :] if c < 8 else ring[:, c, :].rearrange("p (b n) -> p b n", b=2)

        def row_bc(v):
            return v[0:1, :].to_broadcast([P, v.shape[1]])

        @block.sync
        def _(sp):
            def load_block(name, dst, src):
                sp.dma_start(dst, src).then_inc(blk_in[name], 16)

            for j in range(NT):
                sp.dma_start(h[:, j, :], x_v[:, j, :]).then_inc(x_in[j], 16)
            load_block("u", W_U, win_v[:, :, 0:512])
            load_block("va", W_VA, win_v[:, :, 512:1024])
            load_block("v", W_V, win_v[:, :, 2048:2560])
            load_block("q", W_Q, win_v[:, :, 1024:1536])
            load_block("k", W_K, win_v[:, :, 1536:2048])
            load_block("oa", W_OA, wout_v[:, :, 0:512])
            sp.wait_ge(S["unit_done"], 8)
            load_block("ob", W_OB, wout_v[:, :, 512:1024])
            for r in range(3):
                sp.dma_start(bias_raw[r * E:(r + 1) * E, 0:2 * F], b_gu[0]).then_inc(S["bias_in"], 16)
                sp.dma_start(bias_raw[r * E:(r + 1) * E, 2 * F:3 * F], b_dn[0]).then_inc(S["bias_in"], 16)
            sp.wait_ge(S["unit_done"], 12)
            for c in (0, 1):
                sp.dma_start(chunk_dst(c), chunk_src(0, c)).then_inc(arrived[c], 16)
            sp.wait_ge(S["unit_done"], N_PROJ)
            for c in (2, 3, 4, 5):
                sp.dma_start(chunk_dst(c), chunk_src(0, c)).then_inc(arrived[c], 16)
            sp.wait_ge(S["unit_done"], N_SGU)
            sp.dma_start(pnat, p_v).then_inc(S["p_in"], 16)
            sp.wait_ge(S["pv_done"], 32)
            sp.dma_start(wple_sb, wple_v).then_inc(S["wple_in"], 16)
            sp.wait_ge(S["unit_done"], 32)
            sp.wait_ge(S["bias_part"], 3)
            for c in (6, 7, 8, 9, 10, 11):
                sp.dma_start(chunk_dst(c), chunk_src(0, c)).then_inc(arrived[c], 16)

            def load_item(i, e):
                for c in range(NCHUNK):
                    sp.wait_ge(S["chunk_used"], (i - 1) * NCHUNK + c + 1)
                    sp.dma_start(chunk_dst(c), chunk_src(e, c)).then_inc(arrived[c], 16)

            with sp.Fori(1, E) as i:
                load_item(i, i)
            sp.wait_ge(S["route_step"], step("base"))
            nov = sp.value_load(nov_i[0:1, 0:1], min_val=0, max_val=EXTRA)
            with sp.Fori(0, EXTRA) as j:
                with sp.If(j < nov):
                    e = sp.value_load(item_e[0:1, bass.ds(j + E, 1)], min_val=0, max_val=E - 1)
                    load_item(j + E, e)
            sp.wait_ge(S["chunk_used"], (nov + (E - 1)) * NCHUNK + 8)
            sp.dma_start(wpg_sb, wpg_v).then_inc(S["wpg_in"], 16)
            sp.dma_start(gfin, row_bc(g_final.rearrange("(a n) -> a n", a=1))).then_inc(S["gfin_in"], 16)
            sp.wait_ge(S["chunk_used"], (nov + E) * NCHUNK)
            sp.wait_ge(S["scattered_a"], (nov + (E + 1)) * 16)
            sp.wait_ge(S["scattered_b"], (nov + (E + 1)) * 16)
            sp.wait_ge(S["xt_ready"], nov + (E + 1))
            for j in range(NT):
                sp.dma_start(pick[j], picked_v[:, j, :, :]).then_inc(pick_in[j], 16)
            for j in range(NT):
                sp.wait_ge(S["out_ready"], j + 1)
                sp.dma_start(out_v[:, j, :], obuf[:, j % 2, :]).then_inc(out_stored[j], 16)
            for j in range(NT):
                sp.wait_ge(out_stored[j], 16)

        @block.gpsimd
        def _(pool):
            pool.memset(ident[:, :], 0.0).then_inc(S["consts"], 1)
            pool.memset(TU[:, :], 1.0).then_inc(S["consts"], 1)
            pool.memset(mhalf[:, :], -0.5).then_inc(S["consts"], 1)
            pool.wait_ge(S["consts"], 3)
            pool.affine_select(out=ident[:, :], in_=ident[:, :], compare_op=ALU.not_equal, fill=1.0, base=0,
                               pattern=[[-1, P]], channel_multiplier=1).then_inc(S["consts"], 1)
            pool.affine_select(out=tri, in_=tri, compare_op=ALU.is_ge, fill=0.0, base=0,
                               pattern=[[1, P]], channel_multiplier=-1).then_inc(S["consts"], 1)

            def iota(dst, pattern, base_, cm):
                pool.iota(dst, pattern, base=base_, channel_multiplier=cm,
                          allow_small_or_imprecise_dtypes=True).then_inc(S["consts"], 1)

            iota(slots[:, 0, :], [[1, P]], 1, 0)
            iota(slots[:, 1, :], [[0, 2], [1, HALF]], 1, 0)
            pool.memset(eye3[:, :], 0.0).then_inc(S["eye_ready"], 1)
            for n in range(3):
                pool.wait_ge(S["eye_ready"], n + 1)
                pool.affine_select(out=eye3[:, :], in_=eye3[:, :], compare_op=ALU.not_equal, fill=1.0, base=-n * E,
                                   pattern=[[-1, E]], channel_multiplier=1).then_inc(S["eye_ready"], 1)
            iota(eid[:, :], [[1, E]], 0, 0)
            iota(kid[:, :], [[1, TOPK]], 0, 0)
            iota(tok0[:, :], [[P, NT]], -SEQ, 1)
            iota(tok4[:, :], [[P * TOPK, NT]], -SEQ * TOPK, TOPK)
            iota(jt[:, :], [[1, 16]], 0, 0)
            iota(jb[:, :], [[P, 16]], P, 0)
            iota(itemf[:, :], [[1, 48]], 0, 0)

            def power(s, j):
                pool.wait_ge(S["ms_ready"], POW.index((s, j)) + 1)
                pool.tensor_tensor(rstd[:, s, j:j + 1], ms[:, s, j:j + 1], mhalf[:, j:j + 1],
                                   ALU.pow).then_inc(S["rstd_ready"], 1)

            for s_, j in POW[:2 * NT]:
                power(s_, j)
            for n in range(32):
                qb = n % NT
                pool.wait_ge(S["l_ready"], n + 1)
                diag = L[:, n % 2, qb * P:(qb + 1) * P]
                pool.affine_select(out=diag, in_=diag, compare_op=ALU.is_ge, fill=F32_MIN, base=0,
                                   pattern=[[-1, P]], channel_multiplier=1).then_inc(S["l_masked"], 1)
            for s_, j in YH:
                power(s_, j)
                if (s_, j) in ((3, NT - 1), (4, 1)):
                    n = 1 if s_ == 3 else 2
                    rows = slice(0, (3 - n) * E)
                    pool.wait_ge(S["bias_part"], n)
                    pool.tensor_tensor(bias_raw[rows, :], bias_raw[rows, :], bias3[rows, :], ALU.subtract)\
                        .then_inc(S["bias_rest"], 1)

            bound = pool.alloc_register("bound")
            pool.reg_mov(bound, 0)

            def gather(n):
                pool.wait_ge(S["gidx_ready"], n)
                pool.reg_alu(bound, bound, SEQ - 1, ALU.max)
                pool.reg_alu(bound, bound, SEQ - 1, ALU.min)
                pool.indirect_dma_start(xg, None, token_rows, bass.IndirectOffsetOnAxis(gidx, 0),
                                        bounds_check=bound, oob_is_err=False).then_inc(S["gathered"], 16)

            def scatter(i, first=False):
                pool.wait_ge(S["ys_ready"], i + 2)
                if not first:
                    pool.wait_ge(S["cur_ready"], i + 1)
                pool.reg_alu(bound, bound, 2 * SEQ * TOPK - 1, ALU.max)
                for c, done in enumerate(("scattered_a", "scattered_b")):
                    pool.indirect_dma_start(expert_rows, bass.IndirectOffsetOnAxis(scur[:, c:c + 1], 0), ys[:, c, :],
                                            None, bounds_check=bound, oob_is_err=False).then_inc(S[done], 16)

            for j in range(NT):
                pool.wait_ge(xs_stored[j], 16)
            scatter(-1, first=True)
            gather(1)

            def item(i):
                gather(i + 2)
                scatter(i)

            with pool.Fori(0, E) as i:
                item(i)
            nov = pool.value_load(nov_i[0:1, 0:1], min_val=0, max_val=EXTRA)
            with pool.Fori(0, EXTRA) as j:
                with pool.If(j < nov):
                    item(j + E)
            for s_, j in TAIL:
                power(s_, j)

        @block.scalar
        def _(act):
            def row(v):
                return v.rearrange("(r n) -> r n", n=P)

            for r, v in ((V_MIX, row(g_mix[0])), (V_A, row(g_a[0])), (V_B, row(g_b[0])), (V_MOE, row(g_moe[0])),
                         (V_PLE, row(g_ple[0])), (V_BS, b_s[0])):
                act.dma_start(vec_nat[r:r + v.shape[0], :], v).then_inc(S["vec_in"], 16)
            act.dma_start(ws_nat, w_s[0].rearrange("g i j -> i g j")).then_inc(S["ws_in"], 16)
            act.dma_start(wf[:, :, :], win_v[:, :, 2560:2568]).then_inc(S["wf_in"], 16)
            act.dma_start(wr[:, :, :], w_router[0].rearrange("(k p) n -> p k n", p=P)).then_inc(S["wr_in"], 16)
            act.dma_start(bfb[:, :], row_bc(b_f)).then_inc(S["bc_in"], 16)
            act.dma_start(brb[:, :], row_bc(b_router)).then_inc(S["bc_in"], 16)
            act.dma_start(lng, row_bc(ln_g)).then_inc(S["ln_in"], 16)
            act.dma_start(lnb, row_bc(ln_b)).then_inc(S["ln_in"], 16)

            def square(src, s, j, to):
                n = SQ.index((s, j))
                if n >= 2:
                    act.wait_ge(S["sq_ready"], n - 1 if s < 5 else n)
                act.activation(to, src, ACT.Square, accum_out=ss[:, s, j:j + 1]).then_inc(S["sq_ready"], 1)

            for j in range(NT):
                act.wait_ge(x_in[j], 16)
                square(h[:, j, :].rearrange("p (a n) -> p a n", a=2), 0, j,
                       VV[:, 0, 2 * (j % 2):2 * (j % 2) + 2, :])
            act.wait_ge(S["fl_ready"], 2)
            act.activation(fabs[:, :, :], fabs[:, :, :], ACT.Exp).then_inc(S["fexp_ready"], 1)
            act.wait_ge(S["fexp_ready"], 1)
            act.activation(fln[:, :, :], fabs[:, :, :], ACT.Ln, bias=1.0).then_inc(S["fln_ready"], 1)

            def evac(u, dst, func, scale=1.0):
                act.wait_ge(S["unit_done"], u + 1)
                act.activation(dst, bank(4 + u % 2), func, scale=scale).then_inc(S["unit_evac"], 1)

            for j in range(NT):
                evac(2 * j, YC[:, j, 0:512], ACT.Gelu)
                evac(2 * j + 1, VA[:, j, :], ACT.Gelu)
            for j in range(NT):
                evac(8 + j, VT[:, j, :], ACT.Copy)

            def cb_evac(hh):
                act.wait_ge(S["cb_done"], hh + 1)
                if hh >= 2:
                    act.wait_ge(S["l_ready"], 4 * (hh - 1))
                act.activation(Cb[:, hh % 2, :], SM6, ACT.Copy).then_inc(S["cb_ready"], 1)

            def q_evac(pair):
                if pair >= 2:
                    act.wait_ge(S["s_done"], 8 * (pair - 1))
                evac(12 + 2 * pair, QK[:, 0, pair % 2, :], ACT.Copy, scale=HD ** -0.5)

            def softmax_exp(n):
                w = (n % NT + 1) * P
                act.wait_ge(S["max_ready"], n + 1)
                if n >= 2:
                    act.wait_ge(S["pt_done"], n - 1)
                act.activation(Pr[:, n % 2, 0:w], L[:, n % 2, 0:w], ACT.Exp, bias=nmax[:, n:n + 1],
                               accum_out=psumr[:, n:n + 1]).then_inc(S["p_ready"], 1)

            def pt_evac(n):
                w = (n % NT + 1) * P
                act.wait_ge(S["pt_done"], n + 1)
                if n >= 2:
                    act.wait_ge(S["pv_done"], n - 1)
                act.activation(PT[:, n % 2, 0:w], bank(2 + n % 2)[:, 0:w], ACT.Copy).then_inc(S["pt_odd"], 1)

            q_evac(0)
            evac(13, QK[:, 1, 0, :], ACT.Copy)
            cb_evac(0)
            for n in range(33):
                if n % 4 == 1 and n // 4 + 1 < NH:
                    cb_evac(n // 4 + 1)
                if n % 8 == 3 and n < 24:
                    q_evac(n // 8 + 1)
                if n % 8 == 6 and n < 24:
                    evac(15 + 2 * (n // 8), QK[:, 1, (n // 8 + 1) % 2, :], ACT.Copy)
                if n < 32:
                    softmax_exp(n)
                if n >= 1 and (n - 1) % 2:
                    pt_evac(n - 1)
            act.wait_ge(S["sgu_evac"], NG)
            act.wait_ge(S["y_ready"], 32)
            for j in range(NT):
                square(YC[:, j, 0:512], 2, j, L[:, 0, :])
                square(YC[:, j, 512:1024], 3, j, L[:, 1, :])

            def bias_cast(n):
                rows = slice(0, (3 - n) * E)
                if n:
                    act.wait_ge(S["bias_rest"], n)
                act.activation(bias3[rows, :], bias_raw[rows, :], ACT.Copy).then_inc(S["bias_part"], 1)

            act.wait_ge(S["bias_in"], 6 * 16)
            bias_cast(0)
            for j in range(NT):
                act.wait_ge(S["h_ready"], 2 * j + 2)
                square(h[:, j, :], 4, j, scr[:, 0:1024] if j % 2 else scr[:, 1024:2048])
                if j in (0, 2):
                    bias_cast(j // 2 + 1)
                if j >= 1:
                    act.wait_ge(S["xs_ready"], 2 * NT + j)
                    act.dma_start(rows_v[:, j - 1, :], XS[:, (j - 1) % 2, :]).then_inc(xs_stored[j - 1], 16)
            act.wait_ge(S["xs_ready"], 3 * NT)
            act.dma_start(rows_v[:, NT - 1, :], XS[:, (NT - 1) % 2, :]).then_inc(xs_stored[-1], 16)
            act.wait_ge(S["route_step"], step("shift"))
            act.activation(gate4[:, :, :], gate4[:, :, :], ACT.Exp).then_inc(S["gexp_ready"], 1)
            for u in range(8):
                act.wait_ge(S["pw_done"], u + 1)
                act.activation(PW[:, u // 2, (u % 2) * 512:(u % 2) * 512 + 512], bank(u % 2), ACT.Copy)\
                   .then_inc(S["pw_evac"], 1)

            def item(i):
                for c in range(2):
                    act.wait_ge(S["g_ready"], i * 2 + (c + 1))
                    act.activation(sbuf[:, c, :], gbuf[:, c, :], ACT.Sigmoid, scale=ALPHA).then_inc(S["sig_ready"], 1)
                for c in range(2):
                    act.wait_ge(S["atrans_done"], i * 2 + (c + 1))
                    act.activation(XT[:, 6 + c, :], bank(c), ACT.Copy).then_inc(S["at_ready"], 1)
                act.wait_ge(S["chunk_used"], (i + 1) * NCHUNK)
                act.wait_ge(S["cur_ready"], i + 1)
                act.wait_ge(S["scattered_a"], (i + 1) * 16)
                act.wait_ge(S["scattered_b"], (i + 1) * 16)
                act.activation(ys[:, 0, :], bank(6), ACT.Copy, scale=gcur)
                act.activation(ys[:, 1, :], bank(7), ACT.Copy, scale=gcur).then_inc(S["ys_ready"], 1)

            with act.Fori(0, E) as i:
                item(i)
            nov = act.value_load(nov_i[0:1, 0:1], min_val=0, max_val=EXTRA)
            with act.Fori(0, EXTRA) as j:
                with act.If(j < nov):
                    item(j + E)

            def tail_square(s, j):
                if s == 5:
                    act.wait_ge(S["hsum_ready"], j + 1)
                else:
                    act.wait_ge(S["ple_ready"], 2 * j + 2)
                square(h[:, j, :], s, j, junk)

            def gate_sigmoids(j):
                for c in range(2):
                    k = 2 * j + c
                    act.wait_ge(S["unit_done"], 32 + k + 1)
                    if k >= 2:
                        act.wait_ge(S["ple_ready"], k - 1)
                    act.activation(sg[:, c, :], bank(4 + c), ACT.Sigmoid).then_inc(S["sg_ready"], 1)

            for s_, j in TAIL[:2]:
                tail_square(s_, j)
            gate_sigmoids(0)
            tail_square(5, 2)
            tail_square(6, 0)
            gate_sigmoids(1)
            tail_square(5, 3)
            tail_square(6, 1)
            gate_sigmoids(2)
            tail_square(6, 2)
            gate_sigmoids(3)
            tail_square(6, 3)

        @block.tensor
        def _(pe):
            def mm(dst, lhsT, rhs, start, stop, shared=False):
                return pe.matmul(dst, lhsT, rhs, start=start, stop=stop, skip_group_check=shared)

            def transpose_tile(n):
                pe.wait_ge(S["xs_ready"], n + 1)
                if n >= 2:
                    pe.wait_ge(S["tp_evac"], n - 1)
                for k in range(KD):
                    last = pe.transpose(PAIR[n % 2][:, k, :], XS[:, n % 2, k * P:(k + 1) * P], ident[:, :])
                last.then_inc(S["tp_done"], 1)

            pe.wait_ge(S["consts"], 5)
            pe.wait_ge(S["vec_in"], 96)
            pe.transpose(SM6[:, 0:36], vec_nat, ident[0:36, 0:36]).then_inc(S["vecT_done"], 1)
            for j in range(NT):
                transpose_tile(j)
            pe.wait_ge(S["tp_evac"], NT)
            pe.wait_ge(S["ws_in"], 16)
            for g in range(NG):
                last = pe.transpose(bank(2)[:, g * P:(g + 1) * P], ws_nat[:, g, :], ident[:, :])
            last.then_inc(S["ws_done"], 1)
            pe.wait_ge(S["wf_in"], 16)
            pe.wait_ge(S["zero7"], 1)
            for j in range(NT):
                for k in range(KD):
                    last = mm(f_ps[:, j, :], XT[:, k, j * P:(j + 1) * P], wf[:, k, :], k == 0, k == KD - 1)
            last.then_inc(S["f_done"], 1)

            def free_unit(u):
                if 2 <= u < N_PROJ + 2:
                    pe.wait_ge(S["unit_evac"], u - 1)
                elif N_PROJ + 2 <= u < N_SGU + 2:
                    pe.wait_ge(S["sgu_evac"], u - N_PROJ - 1)
                elif N_SGU + 2 <= u < 32:
                    pe.wait_ge(S["h_ready"], u - N_SGU - 1)
                elif u >= 34:
                    pe.wait_ge(S["sg_ready"], u - 33)

            def unit(u, lhsT, rhs, nk=KD, ks=None):
                ks = range(nk) if ks is None else ks
                if ks[0] == 0:
                    free_unit(u)
                for k in ks:
                    last = mm(bank(4 + u % 2), lhsT(k), rhs(k), k == 0, k == nk - 1)
                if ks[-1] == nk - 1:
                    last.then_inc(S["unit_done"], 1)

            def tile_of(j):
                return lambda k: XT[:, k, j * P:(j + 1) * P]

            def cols_of(w, c=None):
                return lambda k: w[:, k, :] if c is None else w[:, k, c * P:(c + 1) * P]

            def all_tokens(k):
                return XT[:, k, :]

            pe.wait_ge(blk_in["u"], 16)
            unit(0, tile_of(0), cols_of(W_U))
            pe.wait_ge(blk_in["va"], 16)
            unit(1, tile_of(0), cols_of(W_VA))
            pe.wait_ge(S["logf_ready"], 1)
            for j in range(NT):
                for i in range(j + 1):
                    last = mm(c_ps[:, j, :], tri if i == j else ones, logf[:, i, :], i == 0, i == j)
            last.then_inc(S["c_done"], 1)
            for j in range(1, NT):
                unit(2 * j, tile_of(j), cols_of(W_U))
                unit(2 * j + 1, tile_of(j), cols_of(W_VA))
            pe.wait_ge(blk_in["v"], 16)
            for j in range(NT):
                unit(8 + j, tile_of(j), cols_of(W_V))
            pe.wait_ge(blk_in["q"], 16)
            unit(12, cols_of(W_Q, 0), all_tokens)
            pe.wait_ge(blk_in["k"], 16)
            unit(13, cols_of(W_K, 0), all_tokens)

            def forget_rows(hh):
                if hh:
                    pe.wait_ge(S["cb_ready"], hh)
                for j in range(NT):
                    last = mm(SM6[:, j * P:SEQ], logf[:, j, hh:hh + 1].to_broadcast([P, P]),
                              TU[:, 0:SEQ - j * P], j == 0, j == NT - 1, True)
                last.then_inc(S["cb_done"], 1)

            def scores(n):
                hh, qb = divmod(n, NT)
                pair, r = divmod(hh, 2)
                if n % 8 == 0:
                    pe.wait_ge(S["unit_evac"], 14 + 2 * pair)
                if n >= 2:
                    pe.wait_ge(S["l_ready"], n - 1)
                mm(bank(n % 2)[:, 0:(qb + 1) * P], QK[r * HD:(r + 1) * HD, 0, pair % 2, qb * P:(qb + 1) * P],
                   QK[r * HD:(r + 1) * HD, 1, pair % 2, 0:(qb + 1) * P], True, True).then_inc(S["s_done"], 1)

            def transpose_probs(n):
                pe.wait_ge(S["p_ready"], n + 1)
                if n >= 2:
                    pe.wait_ge(S["pt_odd" if n % 2 else "pt_even"], n // 2)
                for b in range(n % NT + 1):
                    last = pe.transpose(bank(2 + n % 2)[:, b * P:(b + 1) * P], Pr[:, n % 2, b * P:(b + 1) * P],
                                        ident[:, :])
                last.then_inc(S["pt_done"], 1)

            def values(n):
                hh, qb = divmod(n, NT)
                pe.wait_ge(S["pt_odd" if n % 2 else "pt_even"], n // 2 + 1)
                if n:
                    pe.wait_ge(S["y_ready"], n)
                for b in range(qb + 1):
                    last = mm(o_ps, PT[:, n % 2, b * P:(b + 1) * P], VT[:, b, hh * HD:(hh + 1) * HD],
                              b == 0, b == qb)
                last.then_inc(S["pv_done"], 1)

            pe.wait_ge(S["ctok_ready"], 1)
            pe.wait_ge(S["ws_evac"], 1)
            forget_rows(0)
            SHARE = {0: (0, range(0, 3)), 1: (0, range(3, 6)), 2: (0, range(6, 8)),
                     3: (1, range(0, 3)), 4: (1, range(3, 6)), 5: (1, range(6, 8))}
            for n in range(34):
                if n % 4 == 1 and n // 4 + 1 < NH:
                    forget_rows(n // 4 + 1)
                if n < 32:
                    scores(n)
                if n < 24 and n % 8 in SHARE:
                    kind, ks = SHARE[n % 8]
                    pair = n // 8 + 1
                    unit(12 + 2 * pair + kind, cols_of((W_Q, W_K)[kind], pair), all_tokens, ks=ks)
                if 26 <= n < 30:
                    g = n - 26
                    if g == 0:
                        pe.wait_ge(S["va_ready"], NT)
                    unit(N_PROJ + g, lambda k: wsT[:, g, :], lambda k: VA[:, :, g * P:(g + 1) * P], nk=1)
                if 1 <= n <= 32:
                    transpose_probs(n - 1)
                if n >= 2:
                    values(n - 2)

            def out_projection(j):
                pe.wait_ge(S["tp_evac"], NT + j + 1)
                if j == 0:
                    pe.wait_ge(blk_in["oa"], 16)
                    pe.wait_ge(blk_in["ob"], 16)
                unit(N_SGU + 2 * j, tile_of(j), cols_of(W_OA))
                unit(N_SGU + 2 * j + 1, tile_of(j), cols_of(W_OB))

            transpose_tile(4)
            transpose_tile(5)
            out_projection(0)
            transpose_tile(6)
            out_projection(1)
            transpose_tile(7)
            out_projection(2)
            transpose_tile(8)
            out_projection(3)
            transpose_tile(9)
            transpose_tile(10)
            transpose_tile(11)
            pe.wait_ge(S["tp_evac"], 12)
            pe.wait_ge(S["p_in"], 16)
            for k in range(2):
                for j in range(NT):
                    last = pe.transpose(bank(2 + k)[:, j * P:(j + 1) * P], pnat[:, j, k * P:(k + 1) * P], ident[:, :])
            last.then_inc(S["pT_done"], 1)
            pe.wait_ge(S["wr_in"], 16)
            for j in range(NT):
                for k in range(KD):
                    last = mm(lg_ps[:, j, :], XT[:, k, j * P:(j + 1) * P], wr[:, k, :], k == 0, k == KD - 1)
            last.then_inc(S["lg_done"], 1)
            pe.wait_ge(S["pT_ready"], 1)
            pe.wait_ge(S["wple_in"], 16)

            def ple_product(u):
                j, c = divmod(u, 2)
                if u >= 2:
                    pe.wait_ge(S["pw_evac"], u - 1)
                for k in range(2):
                    last = mm(bank(u % 2), pT[:, k, j * P:(j + 1) * P], wple_sb[:, k, c * 512:(c + 1) * 512],
                              k == 0, k == 1)
                last.then_inc(S["pw_done"], 1)

            for u in range(4):
                ple_product(u)
            pe.wait_ge(S["route_step"], step("mk"))
            for j in range(NT):
                for i in range(j + 1):
                    mm(rank_ps[:, j, :], tri if i == j else ones, Mk[:, i, :], i == 0, i == j)
            for j in range(NT):
                mm(cnt_ps, ones, Mk[:, j, :], j == 0, j == NT - 1)
            for j in range(NT):
                last = mm(cntT_ps, Mk[:, j, :], ones[:, 0:1], j == 0, j == NT - 1)
            last.then_inc(S["rank_done"], 1)
            for u in range(4, 6):
                ple_product(u)
            pe.wait_ge(S["route_step"], step("ext3"))
            mm(xin_ps, extT[:, 2:3].to_broadcast([E, P]), TU[0:E, 0:E], True, True).then_inc(S["xin_done"], 1)
            for u in range(6, 8):
                ple_product(u)

            def list_tokens(n):
                pe.wait_ge(S["sel_ready"], n)
                for j in range(NT):
                    last = mm(idx_ps, selm[:, j, :], dcur[:, j, :], j == 0, j == NT - 1)
                last.then_inc(S["idxmm_done"], 1)

            def transpose_rows(n):
                pe.wait_ge(S["gathered"], n * 16)
                pe.wait_ge(S["places_ready"], n)
                for k in range(KD):
                    last = pe.transpose(T_ps[:, k, :], xg[:, k * P:(k + 1) * P], ident[:, :])
                last.then_inc(S["xtrans_done"], 1)

            def gate_up(k, c, part):
                return ring[:, k, part * F + c * 512:part * F + (c + 1) * 512]

            def gu_bias(c, part):
                return bias3[:, part * F + c * 512:part * F + (c + 1) * 512]

            def down(f, c):
                lo = (f % 2) * D + c * 512
                return ring[:, 8 + f // 2, lo:lo + 512]

            def dn_bias(c):
                return bias3[:, 2 * F + c * 512:2 * F + (c + 1) * 512]

            def lower_upper(c):
                return slice(c * HALF, (c + 1) * HALF)

            def item(i, small):
                def wide(lhsT, rhs, b, c, start, stop):
                    if small:
                        return mm(bank(b)[lower_upper(c), :], lhsT[:, 0:HALF], rhs, start, stop, True)
                    return mm(bank(b), lhsT, rhs, start, stop, True)

                pe.wait_ge(S["xt_ready"], i + 1)
                list_tokens(i + 2)
                pe.wait_ge(S["at_ready"], i * 2 + 1)
                pe.wait_ge(S["act_ready"], i * 2 + 1)
                pieces = [(part, c, part if small else 2 * c + part) for part, c in
                          ([(0, 0), (0, 1), (1, 0), (1, 1)] if small else [(0, 0), (1, 0), (0, 1), (1, 1)])]
                for k in range(KD):
                    pe.wait_ge(arrived[k], (i + 1) * 16)
                    for n, (part, c, b) in enumerate(pieces):
                        last = wide(xTm[:, k, :], gate_up(k, c, part), b, c, k == 0, k == KD - 1)
                        if k == KD - 1 and n == (1 if small else 0):
                            last.then_inc(S["gu_done"], 1)
                        if k == KD - 1 and n in (1, 2) and not small:
                            last.then_inc(S["gu_done"], 1)
                    last.then_inc(S["chunk_used"], 1)
                    if k == 1:
                        pe.wait_ge(S["esel_ready"], i + 1)
                        for part, c, b in pieces:
                            wide(esel[:, :], gu_bias(c, part), b, c, False, False)
                pe.wait_ge(S["ys_ready"], i + 1)
                for c in range(2):
                    last = wide(esel[:, :], dn_bias(c), 6 if small else 6 + c, c, True, False)
                if small:
                    last.then_inc(S["gu_done"], 2)
                transpose_rows(i + 2)
                for c in range(1 if small else 2):
                    pe.wait_ge(S["act_ready"], i * 2 + (c + 2))
                    for f in range(4):
                        last = pe.transpose(bank(c)[:, f * P:(f + 1) * P], ubuf[:, c, f * P:(f + 1) * P], ident[:, :])
                    last.then_inc(S["atrans_done"], 2 if small else 1)
                for f in range(KD):
                    if f % 2 == 0:
                        pe.wait_ge(arrived[8 + f // 2], (i + 1) * 16)
                    if f in (0, 4):
                        pe.wait_ge(S["at_ready"], i * 2 + (2 if small or f == 0 else 3))
                    for c in range(2):
                        if small:
                            last = mm(bank(6)[lower_upper(c), :], aT[:, f % 4, lower_upper(f // 4)], down(f, c),
                                      False, f == KD - 1, True)
                        else:
                            last = mm(bank(6 + c), aT[:, f, :], down(f, c), False, f == KD - 1, True)
                    if f % 2:
                        last.then_inc(S["chunk_used"], 1)

            pe.wait_ge(S["pw_evac"], 8)
            pe.wait_ge(S["route_step"], step("base"))
            pe.wait_ge(S["bias_part"], 3)
            list_tokens(1)
            transpose_rows(1)
            with pe.Fori(0, E) as i:
                small = pe.value_load(item_s[0:1, bass.ds(i, 1)], min_val=0, max_val=1)
                with pe.If(small > 0):
                    item(i, True)
                with pe.Else():
                    item(i, False)
            nov = pe.value_load(nov_i[0:1, 0:1], min_val=0, max_val=EXTRA)
            with pe.Fori(0, EXTRA) as j:
                with pe.If(j < nov):
                    item(j + E, False)
            pe.wait_ge(S["wpg_in"], 16)
            for j in range(NT):
                transpose_tile(12 + j)
                pe.wait_ge(S["tp_evac"], 12 + j + 1)
                for c in range(2):
                    unit(32 + 2 * j + c, tile_of(j), lambda k: wpg_sb[:, k, c * 512:(c + 1) * 512])

        @block.vector
        def _(dve):
            ts, tt, stt = dve.tensor_scalar, dve.tensor_tensor, dve.scalar_tensor_tensor

            def mean_square(s, j, n):
                dve.wait_ge(S["sq_ready"], SQ.index((s, j)) + 1)
                ts(ms[:, s, j:j + 1], ss[:, s, j:j + 1], 1.0 / n, RMS_EPS, ALU.mult, ALU.add)\
                    .then_inc(S["ms_ready"], 1)

            def rstd_of(s, j):
                dve.wait_ge(S["rstd_ready"], POW.index((s, j)) + 1)
                return rstd[:, s, j:j + 1]

            def normalise(n, pieces):
                scales = [(lo, src, rstd_of(s, j)) for lo, src, s, j in pieces]
                if n >= 2:
                    dve.wait_ge(S["tp_done"], n - 1)
                if n in (10, 11):
                    dve.wait_ge(xs_stored[n - 10], 16)
                for lo, src, r in scales:
                    last = ts(XS[:, n % 2, lo:lo + src.shape[1]], src, r, None, ALU.mult)
                last.then_inc(S["xs_ready"], 1)

            def take_transposed(n, v):
                j = n % NT
                dve.wait_ge(S["tp_done"], n + 1)
                tt(XT[:, :, j * P:(j + 1) * P], PAIR[n % 2], spread(vecT[:, v:v + KD], P),
                   ALU.mult).then_inc(S["tp_evac"], 1)

            for lo, hi, m, values in ((0, P, 0, (SEQ, 2 * SEQ * TOPK, 2 * SEQ * TOPK + 1)),
                                      (0, HALF, 1, (SEQ, 2 * SEQ * TOPK, OOB)),
                                      (HALF, P, 1, (OOB, 2 * SEQ * TOPK + 1, OOB))):
                for c, value in enumerate(values):
                    dve.memset(offs[lo:hi, m, c:c + 1], float(value)).then_inc(S["offs_ready"], 1)
            dve.memset(SM7, 0.0).then_inc(S["zero7"], 1)
            dve.wait_ge(S["vecT_done"], 1)
            dve.tensor_copy(vecT[:, :], SM6[:, 0:36]).then_inc(S["vecT_ready"], 1)
            dve.wait_ge(S["vecT_ready"], 1)

            def x_scale(j):
                mean_square(0, j, D)
                normalise(j, [(0, h[:, j, :], 0, j)])

            x_scale(0)
            x_scale(1)
            for j in range(NT):
                take_transposed(j, V_MIX)
                if j + 2 < NT:
                    x_scale(j + 2)
            dve.wait_ge(S["ws_done"], 1)
            dve.tensor_copy(wsT[:, :, :], bank(2).rearrange("p (g i) -> p g i", g=NG)).then_inc(S["ws_evac"], 1)
            dve.wait_ge(S["ws_evac"], 1)
            dve.memset(wsT[64:P, :, 0:64], 0.0).then_inc(S["wsT_ready"], 1)
            dve.wait_ge(S["f_done"], 1)
            dve.wait_ge(S["bc_in"], 32)
            tt(fl[:, :, :], f_ps, stack(bfb[:, :], NT), ALU.add)\
                .then_inc(S["fl_ready"], 1)
            dve.wait_ge(S["fl_ready"], 1)
            stt(fabs[:, :, :], fl[:, :, :], -1.0, fl[:, :, :], ALU.mult, ALU.min).then_inc(S["fl_ready"], 1)
            dve.wait_ge(S["fln_ready"], 1)
            stt(logf[:, :, :], fl[:, :, :], 0.0, fln[:, :, :], ALU.min, ALU.subtract).then_inc(S["logf_ready"], 1)
            dve.wait_ge(S["c_done"], 1)
            dve.tensor_copy(ctok[:, :, :], c_ps).then_inc(S["ctok_ready"], 1)
            dve.wait_ge(S["ln_in"], 32)
            for j in range(NT):
                dve.wait_ge(S["unit_evac"], 2 * j + 2)
                dve.bn_stats(lnst[:, j, :], VA[:, j, :]).then_inc(S["ln_stat"], 1)
                dve.wait_ge(S["ln_stat"], j + 1)
                dve.bn_aggr(lnmv[:, j, :], lnst[:, j, :]).then_inc(S["ln_var"], 1)
                dve.wait_ge(S["ln_var"], j + 1)
                ts(ms[:, 1, j:j + 1], lnmv[:, j, 1:2], LN_EPS, None, ALU.add).then_inc(S["ms_ready"], 1)
                r = rstd_of(1, j)
                ts(VA[:, j, :], VA[:, j, :], lnmv[:, j, 0:1], r, ALU.subtract, ALU.mult).then_inc(S["ln_step"], 1)
                dve.wait_ge(S["ln_step"], 2 * j + 1)
                tt(VA[:, j, :], VA[:, j, :], lng, ALU.mult).then_inc(S["ln_step"], 1)
                dve.wait_ge(S["ln_step"], 2 * j + 2)
                tt(VA[:, j, :], VA[:, j, :], lnb, ALU.add).then_inc(S["va_ready"], 1)

            def logits(n):
                hh, qb = divmod(n, NT)
                w = (qb + 1) * P
                dve.wait_ge(S["s_done"], n + 1)
                dve.wait_ge(S["cb_ready"], hh + 1)
                if n >= 2:
                    dve.wait_ge(S["p_ready"], n - 1)
                stt(L[:, n % 2, 0:w], bank(n % 2)[:, 0:w], ctok[:, qb, hh:hh + 1], Cb[:, hh % 2, 0:w],
                    ALU.add, ALU.subtract).then_inc(S["l_ready"], 1)

            def row_max(n):
                dve.wait_ge(S["l_masked"], n + 1)
                dve.tensor_reduce(nmax[:, n:n + 1], L[:, n % 2, 0:(n % NT + 1) * P], AX, ALU.max, negate=True)\
                    .then_inc(S["max_ready"], 1)

            def take_probs(n):
                w = (n % NT + 1) * P
                dve.wait_ge(S["pt_done"], n + 1)
                if n >= 2:
                    dve.wait_ge(S["pv_done"], n - 1)
                dve.tensor_copy(PT[:, n % 2, 0:w], bank(2 + n % 2)[:, 0:w]).then_inc(S["pt_even"], 1)

            def outputs(n):
                hh, qb = divmod(n, NT)
                dve.wait_ge(S["p_ready"], n + 1)
                dve.reciprocal(rsum[:, n:n + 1], psumr[:, n:n + 1]).then_inc(S["r_ready"], 1)
                dve.wait_ge(S["r_ready"], n + 1)
                dve.wait_ge(S["pv_done"], n + 1)
                ts(YC[:, qb, GW + hh * HD:GW + (hh + 1) * HD], o_ps, rsum[:, n:n + 1], None, ALU.mult)\
                    .then_inc(S["y_ready"], 1)

            for n in range(35):
                if n < 32:
                    logits(n)
                if 1 <= n <= 32:
                    row_max(n - 1)
                if 2 <= n < 34 and n % 2 == 0:
                    take_probs(n - 2)
                if n >= 3:
                    outputs(n - 3)
                if 27 <= n < 31:
                    g = n - 27
                    cols = YC[:, :, g * P:(g + 1) * P]
                    dve.wait_ge(S["unit_done"], N_PROJ + g + 1)
                    stt(cols, bank(4 + g % 2).rearrange("p (j c) -> p j c", j=NT), vecT[:, V_BS + g:V_BS + g + 1],
                        cols, ALU.add, ALU.mult).then_inc(S["sgu_evac"], 1)

            def y_scale(j):
                mean_square(2, j, GW)
                mean_square(3, j, FW)
                normalise(4 + j, [(0, YC[:, j, 0:GW], 2, j), (GW, YC[:, j, GW:D], 3, j)])

            def residual(j):
                for c in range(2):
                    u = N_SGU + 2 * j + c
                    dve.wait_ge(S["unit_done"], u + 1)
                    tt(h[:, j, c * 512:(c + 1) * 512], h[:, j, c * 512:(c + 1) * 512], bank(4 + c), ALU.add)\
                        .then_inc(S["h_ready"], 1)

            def h_scale(j):
                mean_square(4, j, D)
                normalise(8 + j, [(0, h[:, j, :], 4, j)])

            y_scale(0)
            y_scale(1)
            take_transposed(4, V_A)
            y_scale(2)
            take_transposed(5, V_A)
            residual(0)
            y_scale(3)
            take_transposed(6, V_A)
            residual(1)
            take_transposed(7, V_A)
            h_scale(0)
            residual(2)
            h_scale(1)
            take_transposed(8, V_MOE)
            residual(3)
            h_scale(2)
            take_transposed(9, V_MOE)
            h_scale(3)
            take_transposed(10, V_MOE)
            take_transposed(11, V_MOE)
            dve.wait_ge(S["pT_done"], 1)
            dve.tensor_copy(pT, bank(2, 2).rearrange("p (k t) -> p k t", k=2)).then_inc(S["pT_ready"], 1)

            def r(name, ins, wait=True):
                ins.then_inc(S["route_step"], 1)
                if wait:
                    dve.wait_ge(S["route_step"], step(name))

            dve.wait_ge(S["lg_done"], 1)
            r("bias", tt(lg[:, :, :], lg_ps, stack(brb[:, :], NT),
                         ALU.add))
            for j in range(NT):
                r(f"max{j}", dve.max(top[:, j, :], lg[:, j, :]))
            for j in range(NT):
                r(f"arg{j}", dve.max_index(topi[:, j, :], top[:, j, :], lg[:, j, :]))
            r("argf", dve.tensor_copy(topf[:, :, :], topi[:, :, :]))
            r("shift", tt(gate4[:, :, :], top[:, :, 0:TOPK], top[:, :, 0:1].to_broadcast([P, NT, TOPK]), ALU.subtract))
            dve.wait_ge(S["gexp_ready"], 1)
            r("gsum", dve.tensor_reduce(gsum[:, :], gate4[:, :, :], AX, ALU.add))
            r("grcp", dve.reciprocal(gsum[:, :], gsum[:, :]))
            r("gates", tt(gate4[:, :, :], gate4[:, :, :],
                          spread(gsum[:, :], TOPK), ALU.mult))
            for k in range(TOPK):
                last = tt(eq[:, k], topf[:, :, k:k + 1].to_broadcast([P, NT, E]),
                          stack(eid[:, :], NT), ALU.is_equal)
            r("eq", last)
            r("mk", dve.tensor_reduce(Mk[:, :, :], eq.rearrange("p k j e -> p j e k"), AX, ALU.add))
            for k in range(TOPK):
                last = tt(wq[:, k], eq[:, k], gate4[:, :, k:k + 1].to_broadcast([P, NT, E]), ALU.mult)
            r("wgate", last)
            r("gk", dve.tensor_reduce(dest[:, :, :, 2], wq.rearrange("p k j e -> p j e k"), AX, ALU.add))
            for k in range(TOPK):
                last = ts(wq2[:, k], eq[:, k], float(k), None, ALU.mult)
            r("wrank", last)
            r("qk", dve.tensor_reduce(dest[:, :, :, 1], wq2.rearrange("p k j e -> p j e k"), AX, ALU.add))
            r("dest0", tt(dest[:, :, :, 1], dest[:, :, :, 1],
                          spread(tok4[:, :], E), ALU.add))
            r("dest1", dve.tensor_copy(dest[:, :, :, 0],
                                       spread(tok0[:, :], E)))
            dve.wait_ge(S["rank_done"], 1)
            r("c1", tt(R1[:, :, :], rank_ps, Mk[:, :, :], ALU.mult))
            r("cnt", dve.tensor_copy(cntB[:, :], cnt_ps))
            r("ext1", ts(extT[:, 0:1], cntT_ps, float(P), None, ALU.is_gt))
            r("ext2", stt(extT[:, 1:2], cntT_ps, 2.0 * P, extT[:, 0:1], ALU.is_gt, ALU.add))
            r("ext3", stt(extT[:, 2:3], cntT_ps, 3.0 * P, extT[:, 1:2], ALU.is_gt, ALU.add))
            dve.wait_ge(S["xin_done"], 1)
            xrow = stack(xin[:, :], 16)
            r("xin", dve.tensor_copy(xin[:, :], xin_ps))
            r("cmp", tt(ovc, xrow, spread(jt[:, :], E), ALU.is_le))
            r("ecount", dve.tensor_reduce(itemf[:, E:48], ovc, AX, ALU.add))
            r("val", tt(ovv, ovc, xrow, ALU.mult))
            r("vmax", dve.tensor_reduce(ovm[:, :], ovv, AX, ALU.max))
            r("clip", ts(itemf[:, E:48], itemf[:, E:48], float(E - 1), None, ALU.min))
            r("base0", dve.memset(base[:, 0:E], 0.0))
            r("vneg", ts(ovm[:, :], ovm[:, :], -float(P), None, ALU.mult))
            r("base1", tt(base[:, E:48], ovm[:, :], jb[:, :], ALU.add))
            r("item_e", dve.tensor_copy(item_e[:, :], itemf[0:1, :]))
            r("small0", dve.memset(item_s[:, :], 0))
            r("small1", ts(item_s[:, 0:E], cntB[0:1, :], float(HALF), None, ALU.is_le))
            r("nov_i", dve.tensor_copy(nov_i[:, :], xin[0:1, E - 1:E]))
            r("base", dve.memset(xg, 0.0))

            def select(i, n):
                e = dve.value_load(item_e[0:1, bass.ds(i, 1)], min_val=0, max_val=E - 1)
                small = dve.value_load(item_s[0:1, bass.ds(i, 1)], min_val=0, max_val=1)
                dve.tensor_copy(ocur, offs[:, bass.ds(small, 1), :].rearrange("p a t -> p (a t)"))
                for j in range(NT):
                    ts(selm[:, j, :], slots[:, bass.ds(small, 1), :].rearrange("p a s -> p (a s)"),
                       base[:, bass.ds(i, 1)], R1[:, j, bass.ds(e, 1)], ALU.add, ALU.is_equal)
                for j in range(NT):
                    last = dve.tensor_copy(dcur[:, j, :], dest[:, j, bass.ds(e, 1), :].rearrange("p a t -> p (a t)"))
                last.then_inc(S["sel_ready"], 1)
                return e

            def take_tokens(n):
                dve.wait_ge(S["idxmm_done"], n)
                tt(gidx, idx_ps[:, 0:1], ocur[:, 0:1], ALU.add).then_inc(S["gidx_ready"], 1)

            def take_places(n):
                dve.tensor_copy(gnext, idx_ps[:, 2:3])
                stt(snext, idx_ps[:, 1:2].to_broadcast([P, 2]), 2.0, ocur[:, 1:3], ALU.mult, ALU.add)\
                    .then_inc(S["places_ready"], 1)

            def take_rows(e, n):
                dve.wait_ge(S["xtrans_done"], n)
                tt(xTm, T_ps, spread(vecT[:, V_MOE:V_MOE + KD], P), ALU.mult).then_inc(S["xt_ready"], 1)
                dve.tensor_copy(esel[:, :], eye3[:, bass.ds(e, 1)].to_broadcast([3 * E, P])).then_inc(S["esel_ready"], 1)

            def item(i):
                e = select(i + 1, i + 2)
                take_tokens(i + 2)
                dve.wait_ge(S["ys_ready"], i + 1)
                dve.wait_ge(S["scattered_a"], (i + 1) * 16)
                dve.wait_ge(S["scattered_b"], (i + 1) * 16)
                dve.wait_ge(S["places_ready"], i + 1)
                dve.tensor_copy(gcur, gnext)
                dve.tensor_copy(scur, snext).then_inc(S["cur_ready"], 1)
                dve.wait_ge(S["cur_ready"], i + 1)
                take_places(i + 2)
                for c in range(2):
                    dve.wait_ge(S["gu_done"], i * 3 + (1 + 2 * c))
                    ts(gbuf[:, c, :], bank(2 * c), LIMIT, None, ALU.min).then_inc(S["g_ready"], 1)
                    if c == 0:
                        dve.wait_ge(S["gu_done"], i * 3 + 2)
                    else:
                        dve.wait_ge(S["chunk_used"], i * NCHUNK + 8)
                    ts(ubuf[:, c, :], bank(2 * c + 1), LIMIT, -LIMIT, ALU.min, ALU.max).then_inc(S["u_ready"], 1)
                    dve.wait_ge(S["u_ready"], i * 2 + (c + 1))
                    stt(ubuf[:, c, :], ubuf[:, c, :], 1.0, gbuf[:, c, :], ALU.add, ALU.mult).then_inc(S["a_ready"], 1)
                    dve.wait_ge(S["a_ready"], i * 2 + (c + 1))
                    dve.wait_ge(S["sig_ready"], i * 2 + (c + 1))
                    tt(ubuf[:, c, :], ubuf[:, c, :], sbuf[:, c, :], ALU.mult).then_inc(S["act_ready"], 1)
                take_rows(e, i + 2)

            dve.memset(ahead[:, 0:1], 0.0).then_inc(S["at_ready"], 1)
            dve.memset(ahead[:, 1:2], 0.0).then_inc(S["act_ready"], 1)
            dve.memset(scur, OOB)
            dve.memset(ys, 0.0).then_inc(S["ys_ready"], 1)
            dve.wait_ge(S["offs_ready"], 9)
            dve.wait_ge(S["eye_ready"], 4)
            e = select(0, 1)
            take_tokens(1)
            take_places(1)
            take_rows(e, 1)
            with dve.Fori(0, E) as i:
                item(i)
            nov = dve.value_load(nov_i[0:1, 0:1], min_val=0, max_val=EXTRA)
            with dve.Fori(0, EXTRA) as j:
                with dve.If(j < nov):
                    item(j + E)

            def sum_rows(j):
                t = pick[j]
                dve.wait_ge(pick_in[j], 16)
                tt(t[:, 0:2, :], t[:, 0:2, :], t[:, 2:4, :], ALU.add).then_inc(S["sum_step"], 1)
                dve.wait_ge(S["sum_step"], 2 * j + 1)
                tt(t[:, 0, :], t[:, 0, :], t[:, 1, :], ALU.add).then_inc(S["sum_step"], 1)
                dve.wait_ge(S["sum_step"], 2 * j + 2)
                tt(h[:, j, :], h[:, j, :], t[:, 0, :], ALU.add).then_inc(S["hsum_ready"], 1)

            def ple_scale(j):
                normalise(12 + j, [(0, h[:, j, :], 5, j)])
                take_transposed(12 + j, V_PLE)

            def add_ple(j):
                for c in range(2):
                    k, cols = 2 * j + c, slice(c * 512, (c + 1) * 512)
                    dve.wait_ge(S["sg_ready"], k + 1)
                    tt(sg[:, c, :], sg[:, c, :], PW[:, j, cols], ALU.mult).then_inc(S["ple_step"], 1)
                    dve.wait_ge(S["ple_step"], k + 1)
                    tt(h[:, j, cols], h[:, j, cols], sg[:, c, :], ALU.add).then_inc(S["ple_ready"], 1)

            def final(j):
                sc = rstd_of(6, j)
                dve.wait_ge(S["gfin_in"], 16)
                if j >= 2:
                    dve.wait_ge(out_stored[j - 2], 16)
                stt(obuf[:, j % 2, :], h[:, j, :], sc, gfin, ALU.mult, ALU.mult).then_inc(S["out_ready"], 1)

            sum_rows(0)
            mean_square(5, 0, D)
            sum_rows(1)
            mean_square(5, 1, D)
            ple_scale(0)
            sum_rows(2)
            mean_square(5, 2, D)
            ple_scale(1)
            add_ple(0)
            mean_square(6, 0, D)
            sum_rows(3)
            mean_square(5, 3, D)
            ple_scale(2)
            add_ple(1)
            final(0)
            mean_square(6, 1, D)
            ple_scale(3)
            add_ple(2)
            final(1)
            mean_square(6, 2, D)
            add_ple(3)
            final(2)
            mean_square(6, 3, D)
            final(3)


_INS = ["x", "p", "g_mix", "w_in", "ln_g", "ln_b", "w_s", "b_s", "b_f", "g_a", "g_b", "w_out", "g_moe", "w_router",
        "b_router", "w_gu", "b_gu", "w_dn", "b_dn", "g_ple", "w_ple_gate", "w_ple", "g_final"]


def kernel(**inputs):
    import numpy as np
    import concourse.bacc as bacc
    from concourse import mybir as mb
    from concourse.bass_utils import run_bass_kernel_spmd as run

    nc = bacc.Bacc("TRN2", target_bir_lowering=False, num_devices=1)
    arrays, args = {}, []
    for name in _INS:
        a = np.ascontiguousarray(inputs[name])
        arrays[f"in_{name}"] = a
        args.append(nc.dram_tensor(f"in_{name}", a.shape, mb.dt.from_np(a.dtype), kind="ExternalInput").ap())
    o = nc.dram_tensor("out_0", (1, SEQ, D), mb.dt.float32, kind="ExternalOutput").ap()
    build(nc, *args, o)
    r = run(nc, [arrays], core_ids=[0])
    return r.results[0]["out_0"]
```

```python
import concourse.bass as bass
from concourse import mybir
from contextlib import ExitStack

P = 128
SEQ, D = 512, 1024
NT, KD = SEQ // P, D // P
GW, FW, PLE = 512, 512, 256
NH, HD = 8, 64
NG = 4
E, TOPK, F = 32, 4, 1024
EXTRA = 15
BANK = 512
NCHUNK = 12
RMS_EPS, LN_EPS = 1e-5, 1e-5
LIMIT, ALPHA = 7.0, 1.702
F32_MIN = -3.4028234663852886e38
OOB = 16384
HALF, QUARTER = P // 2, P // 4
LARGE, MEDIUM, SMALL = 0, 1, 2


def build(nc, x, p, g_mix, w_in, ln_g, ln_b, w_s, b_s, b_f, g_a, g_b, w_out, g_moe, w_router,
          b_router, w_gu, b_gu, w_dn, b_dn, g_ple, w_ple_gate, w_ple, g_final, out):
    fp32, bf16, i32, u32 = mybir.dt.float32, mybir.dt.bfloat16, mybir.dt.int32, mybir.dt.uint32
    ALU = mybir.AluOpType
    ACT = mybir.ActivationFunctionType
    AX = mybir.AxisListType.X

    token_rows = nc.dram_tensor("token_rows", [SEQ, D], fp32).ap()
    sums = nc.dram_tensor("sums", [SEQ * 2, D // 2], fp32).ap()

    x_v = x[0].rearrange("(j p) d -> p j d", p=P)
    out_v = out[0].rearrange("(j p) d -> p j d", p=P)
    p_v = p[0, 0].rearrange("(j p) d -> p j d", p=P)
    win_v = w_in[0].rearrange("(k p) n -> p k n", p=P)
    wout_v = w_out[0].rearrange("(k p) n -> p k n", p=P)
    wpg_v = w_ple_gate[0].rearrange("(k p) n -> p k n", p=P)
    wple_v = w_ple[0].rearrange("(k p) n -> p k n", p=P)
    rows_v = token_rows.rearrange("(j p) d -> p j d", p=P)
    sums_q = sums.rearrange("r (c d) -> (r c) d", c=2)
    sums_v = sums.rearrange("(j p c) d -> p j (c d)", p=P, c=2)

    ctx = ExitStack()
    with ctx:
        def sb(name, shape, dt=fp32):
            return ctx.enter_context(nc.sbuf_tensor(name, shape, dt))

        def sem(name):
            return ctx.enter_context(nc.semaphore(name))

        ring = sb("ring", [P, NCHUNK, 2048])
        h = sb("h", [P, NT, D])
        XT = sb("XT", [P, KD, SEQ])
        YC = sb("YC", [P, NT, D])
        VV = sb("VV", [P, 2, NT, 512])
        XS = sb("XS", [P, 2, D])
        QK = sb("QK", [P, 2, 2, 512])
        scr = sb("scr", [P, 4096])
        quarters = scr[:, 1024:1536]
        VA, VT = VV[:, 0], VV[:, 1]
        L = scr[:, 0:1024].rearrange("p (b n) -> p b n", b=2)
        Pr = scr[:, 1024:2048].rearrange("p (b n) -> p b n", b=2)
        PT = scr[:, 2048:3072].rearrange("p (b n) -> p b n", b=2)
        Cb = scr[:, 3072:4096].rearrange("p (b n) -> p b n", b=2)
        bias_raw = ring[0:3 * E, 10:12, :].rearrange("p a n -> p (a n)")[:, 0:3 * F]
        bias3 = scr[0:3 * E, 2560:4096].bitcast(bf16)
        vec_nat = scr[0:36, 3072:3200]
        ws_nat = YC[:, 0, 512:1024].rearrange("p (g j) -> p g j", g=NG)
        lng, lnb = XS[:, 0, 0:512], XS[:, 1, 0:512]
        ident = sb("ident", [P, P])
        TU = sb("TU", [P, SEQ])
        tri, ones = TU[:, 0:P], TU[:, P:2 * P]
        slot1 = sb("slot1", [P, P])
        dup = sb("dup", [P, 2, P])
        offs = sb("offs", [P, 3, 3])
        eye4 = sb("eye4", [P, E])
        eye3 = sb("eye3", [3 * E, E], bf16)
        esel = sb("esel", [3 * E, P], bf16)
        vecT = sb("vecT", [P, 36])
        wsT = sb("wsT", [P, NG, P])
        wr = sb("wr", [P, KD, E])
        wf = VV[:, 1, 0, 0:KD * NH].rearrange("p (k n) -> p k n", k=KD)
        bfb = sb("bfb", [P, NH])
        brb = sb("brb", [P, E])
        mhalf = sb("mhalf", [P, NT])
        ss = sb("ss", [P, 7, NT])
        ms = sb("ms", [P, 7, NT])
        rstd = sb("rstd", [P, 7, NT])
        lnst = sb("lnst", [P, NT, 6])
        lnmv = sb("lnmv", [P, NT, 2])
        fl = sb("fl", [P, NT, NH])
        fabs = sb("fabs", [P, NT, NH])
        fln = sb("fln", [P, NT, NH])
        logf = sb("logf", [P, NT, NH])
        ctok = sb("ctok", [P, NT, NH])
        nmax = sb("nmax", [P, 32])
        psumr = sb("psumr", [P, 32])
        rsum = sb("rsum", [P, 32])
        lg = sb("lg", [P, NT, E])
        top = sb("top", [P, NT, 8])
        topi = sb("topi", [P, NT, 8], u32)
        topf = sb("topf", [P, NT, 8])
        gate4 = sb("gate4", [P, NT, TOPK])
        gsum = sb("gsum", [P, NT])
        eid = sb("eid", [P, E])
        eq = Pr[:, 0, :].rearrange("p (k j e) -> p k j e", k=TOPK, j=NT)
        wq = Pr[:, 1, :].rearrange("p (k j e) -> p k j e", k=TOPK, j=NT)
        Mk = sb("Mk", [P, NT, E])
        R1 = sb("R1", [P, NT, E])
        Gk = sb("Gk", [P, NT, E])
        tok0 = sb("tok0", [P, NT])
        cntB = sb("cntB", [P, E])
        extT = sb("extT", [E, 3])
        xin = sb("xin", [P, E])
        jt = sb("jt", [P, 16])
        jb = sb("jb", [P, 16])
        ovc = XT[:, 0, :].rearrange("p (j e) -> p j e", e=E)
        ovv = XT[:, 1, :].rearrange("p (j e) -> p j e", e=E)
        ovm = sb("ovm", [P, 16])
        base = sb("base", [P, 48])
        itemf = sb("itemf", [P, 48])
        item_e = sb("item_e", [1, 48], i32)
        kind_i = sb("kind_i", [1, 48], i32)
        nov_i = sb("nov_i", [1, 1], i32)
        xg = scr[:, 0:D]
        selm = scr[:, 1536:2048].rearrange("p (j s) -> p j s", j=NT)
        dcur = scr[:, 2048:2056].rearrange("p (j t) -> p j t", j=NT)
        ocur = scr[:, 2064:2067]
        lcur = scr[:, 2068:2070]
        gcur = scr[:, 2088:2090].rearrange("p (a b) -> p a b", b=1)
        gidx = scr[:, 2090:2091].bitcast(u32)
        scur = scr[:, 2092:2095].bitcast(u32)
        at_most_half = scr[0:1, 2110:2110 + E]
        ahead = scr[:, 2100:2102]
        pnat = VV[:, 0, 2:4, :].rearrange("p a n -> p (a n)").rearrange("p (j d) -> p j d", j=NT)
        pT = QK[:, 0, :, :]
        gbuf, ubuf, sbuf = XT[:, 0:2, :], XT[:, 2:4, :], XT[:, 4:6, :]
        aT = XT[:, 6:8, :].rearrange("p a (b s) -> p (a b) s", b=4)
        ys = QK[:, 1, :, :]
        xTm = VV[:, 0, 0:2, :].rearrange("p a (b s) -> p (a b) s", b=4)
        wple_sb = VV[:, 1, :, :].rearrange("p a n -> p (a n)").rearrange("p (k n) -> p k n", k=2)
        PW = YC
        wpg_sb = ring[:, 0:4, :].rearrange("p a (b n) -> p (a b) n", b=2)
        gfin = ring[:, 5, 0:D]
        obuf = ring[:, 4, :].rearrange("p (b n) -> p b n", b=2)
        sg = QK[:, 0, :, :]
        junk = QK[:, 1, :, :].rearrange("p a n -> p (a n)")

        PS = ctx.enter_context(nc.psum_tensor("PS", [P, 8 * BANK], fp32))

        def bank(b, n=1):
            return PS[:, b * BANK:(b + n) * BANK]

        PAIR = [bank(0, 2).rearrange("p (k t) -> p k t", k=KD), bank(2, 2).rearrange("p (k t) -> p k t", k=KD)]
        SM6, SM7 = bank(6), bank(7)
        c_ps = SM7[:, 64:96].rearrange("p (j h) -> p j h", j=NT)
        f_ps = SM6[:, 64:96].rearrange("p (j h) -> p j h", j=NT)
        o_ps = SM7[:, 128:192]
        lg_ps = SM6[:, 0:128].rearrange("p (j e) -> p j e", j=NT)
        rank_ps = SM7[:, 0:128].rearrange("p (j e) -> p j e", j=NT)
        cnt_ps = SM7[:, 128:160]
        cntT_ps = SM7[0:E, 160:161]
        xin_ps = SM6[:, 256:288]
        T_ps = bank(4, 2).rearrange("p (k s) -> p k s", s=P)
        idx_ps = bank(5)[:, 0:2]
        dup_ps = bank(4)[:, 0:4].rearrange("p (a t) -> p a t", a=2)

        def ple_bank(u):
            return bank(u % 2 + (6 if u < 5 else 0))

        V_MIX, V_A, V_B, V_MOE, V_PLE, V_BS = 0, 8, 12, 16, 24, 32
        def block_at(s):
            return ring[:, s:s + 2, :].rearrange("p a (b n) -> p (a b) n", b=4)
        W_U, W_VA, W_V, W_Q, W_K, W_OA, W_OB = (block_at(s) for s in (8, 10, 0, 2, 4, 6, 0))

        TAIL = [(5, j) for j in range(NT)] + [(6, j) for j in range(NT)]
        YH = [(s, j) for j in range(NT) for s in (2, 3)] + [(4, j) for j in range(NT)]
        SQ = [(0, j) for j in range(NT)] + YH + TAIL
        POW = [(s, j) for s in (0, 1) for j in range(NT)] + YH + TAIL
        ROUTE = ("bias max0 max1 max2 max3 arg0 arg1 arg2 arg3 argf shift gsum grcp gates eq mk wgate gk "
                 "tok e_first base0 kind0 c1 cnt kind1 kind2 "
                 "ext1 ext2 ext3 xin cmp ecount val vmax clip vneg base1 item_e nov_i").split()

        def step(name):
            return ROUTE.index(name) + 1

        def spread(v, n):
            return v.rearrange("p (m a) -> p m a", a=1).to_broadcast([P, v.shape[1], n])

        def stack(v, n):
            return v.rearrange("p (a m) -> p a m", a=1).to_broadcast([P, n, v.shape[1]])

        names = """consts vec_in bias_in ws_in bc_in ln_in wr_in wf_in
            sq_ready ms_ready rstd_ready xs_ready tp_done tp_evac
            vecT_done vecT_ready  ws_done ws_evac bias_part bias_rest eye_ready
            unit_done unit_evac sgu_evac h_ready
            fpart_done fpart_ready lpart_done lpart_ready f_done fl_ready fexp_ready fln_ready logf_ready c_done ctok_ready
            va_gelu u_gelu ln_stat ln_var ln_step va_ready
            cb_done cb_ready s_done l_ready l_masked max_ready p_ready pt_done pt_even pt_odd pv_done r_ready y_ready
            lg_done route_step gexp_ready rank_done cnt_done xin_done
            p_in pT_done pT_ready pw_done pw_evac wple_in
            sel_ready idxmm_done gidx_ready list_ready dup_done ocur_ready xtrans_done xt_ready esel_ready offs_ready
            gu_done g_ready u_ready a_ready act_ready sig_ready atrans_done at_ready
            ys_ready cur_ready xg_clear h_stored gathered scattered_a scattered_b scattered_c dup_ready chunk_used
            zero7 sg_ready ple_step ple_ready out_ready wpg_in gfin_in""".split()
        S = {n: sem(n) for n in names}
        x_in = [sem(f"x_in{j}") for j in range(NT)]
        blk_in = {n: sem(f"blk_{n}") for n in ("u", "va", "v", "q", "k", "oa", "ob")}
        arrived = [sem(f"arrived{c}") for c in range(NCHUNK)]
        xs_stored = [sem(f"xs_stored{j}") for j in range(NT)]
        out_stored = [sem(f"out_stored{j}") for j in range(NT)]
        sum_in = [sem(f"sum_in{j}") for j in range(NT)]

        block = ctx.enter_context(nc.Block())

        N_PROJ, N_SGU = 20, 24
        FILL = [("q", 1), ("k", 1), ("va", 0), ("va", 1), ("q", 2), ("k", 2), ("va", 2), ("va", 3),
                ("q", 3), ("k", 3), ("u", 0), ("u", 1), ("u", 2), ("u", 3)]

        def fill_unit(kind, j):
            return 6 + FILL.index((kind, j))

        def fill_of(n):
            return range(4 * n, 4 * n + 4) if n < 16 else range(3 * n + 16, 3 * n + 19)

        def filled_before(n):
            return [FILL[i // KD] for i in (fill_of(n - 1) if 1 <= n <= 32 else ()) if i % KD == KD - 1]
        LN_AT, LN_FROM = 19, 21

        def chunk_src(e, c):
            if c < 8:
                return w_gu[0, e, c * P:(c + 1) * P, :]
            r = (c - 8) * 2 * P
            return w_dn[0, e, r:r + 2 * P, :].rearrange("(b p) n -> p b n", p=P)

        def chunk_dst(c):
            return ring[:, c, :] if c < 8 else ring[:, c, :].rearrange("p (b n) -> p b n", b=2)

        def row_bc(v):
            return v[0:1, :].to_broadcast([P, v.shape[1]])

        @block.sync
        def _(sp):
            def load_block(name, dst, src):
                sp.dma_start(dst, src).then_inc(blk_in[name], 16)

            for j in range(NT):
                sp.dma_start(h[:, j, :], x_v[:, j, :]).then_inc(x_in[j], 16)
            sp.dma_start(ws_nat, w_s[0].rearrange("g i j -> i g j")).then_inc(S["ws_in"], 16)
            sp.dma_start(wf[:, :, :], win_v[:, :, 2560:2568]).then_inc(S["wf_in"], 16)
            sp.wait_ge(S["vec_in"], 96)
            sp.wait_ge(S["wf_in"], 16)
            sp.wait_ge(S["ws_in"], 16)
            load_block("v", W_V, win_v[:, :, 2048:2560])
            load_block("q", W_Q, win_v[:, :, 1024:1536])
            load_block("k", W_K, win_v[:, :, 1536:2048])
            load_block("va", W_VA, win_v[:, :, 512:1024])
            sp.wait_ge(S["tp_done"], NT)
            sp.dma_start(lng, row_bc(ln_g)).then_inc(S["ln_in"], 16)
            sp.dma_start(lnb, row_bc(ln_b)).then_inc(S["ln_in"], 16)
            load_block("u", W_U, win_v[:, :, 0:512])
            load_block("oa", W_OA, wout_v[:, :, 0:512])
            sp.wait_ge(S["unit_done"], 4)
            load_block("ob", W_OB, wout_v[:, :, 512:1024])
            sp.wait_ge(S["unit_done"], fill_unit("va", 3) + 1)
            for r in range(3):
                sp.dma_start(bias_raw[r * E:(r + 1) * E, 0:2 * F], b_gu[0]).then_inc(S["bias_in"], 16)
                sp.dma_start(bias_raw[r * E:(r + 1) * E, 2 * F:3 * F], b_dn[0]).then_inc(S["bias_in"], 16)
            sp.wait_ge(S["unit_done"], fill_unit("k", 3) + 1)
            for c in (2, 3, 4, 5):
                sp.dma_start(chunk_dst(c), chunk_src(0, c)).then_inc(arrived[c], 16)
            sp.wait_ge(S["unit_done"], N_PROJ)
            for c in (8, 9):
                sp.dma_start(chunk_dst(c), chunk_src(0, c)).then_inc(arrived[c], 16)
            sp.wait_ge(S["unit_done"], N_SGU)
            sp.dma_start(pnat, p_v).then_inc(S["p_in"], 16)
            sp.wait_ge(S["pv_done"], 32)
            sp.dma_start(wple_sb, wple_v).then_inc(S["wple_in"], 16)
            sp.wait_ge(S["unit_done"], 32)
            for c in (0, 1, 6, 7):
                sp.dma_start(chunk_dst(c), chunk_src(0, c)).then_inc(arrived[c], 16)
            sp.wait_ge(S["bias_part"], 3)
            for c in (10, 11):
                sp.dma_start(chunk_dst(c), chunk_src(0, c)).then_inc(arrived[c], 16)

            def load_item(i, e):
                for c in range(NCHUNK):
                    sp.wait_ge(S["chunk_used"], (i - 1) * NCHUNK + c + 1)
                    sp.dma_start(chunk_dst(c), chunk_src(e, c)).then_inc(arrived[c], 16)

            with sp.Fori(1, E) as i:
                load_item(i, i)
            sp.wait_ge(S["route_step"], step("nov_i"))
            nov = sp.value_load(nov_i[0:1, 0:1], min_val=0, max_val=EXTRA)
            with sp.Fori(0, EXTRA) as j:
                with sp.If(j < nov):
                    e = sp.value_load(item_e[0:1, bass.ds(j + E, 1)], min_val=0, max_val=E - 1)
                    load_item(j + E, e)
            sp.wait_ge(S["chunk_used"], (nov + (E - 1)) * NCHUNK + 8)
            sp.dma_start(wpg_sb, wpg_v).then_inc(S["wpg_in"], 16)
            sp.dma_start(gfin, row_bc(g_final.rearrange("(a n) -> a n", a=1))).then_inc(S["gfin_in"], 16)
            sp.wait_ge(S["chunk_used"], (nov + E) * NCHUNK)
            sp.wait_ge(S["scattered_a"], (nov + (E + 1)) * 16)
            sp.wait_ge(S["scattered_b"], (nov + (E + 1)) * 16)
            sp.wait_ge(S["scattered_c"], (nov + (E + 1)) * 16)
            for j in range(NT):
                sp.dma_start(h[:, j, :], sums_v[:, j, :]).then_inc(sum_in[j], 16)
            for j in range(NT):
                sp.wait_ge(S["out_ready"], j + 1)
                sp.dma_start(out_v[:, j, :], obuf[:, j % 2, :]).then_inc(out_stored[j], 16)
            for j in range(NT):
                sp.wait_ge(out_stored[j], 16)

        @block.gpsimd
        def _(pool):
            pool.memset(ident[:, :], 0.0).then_inc(S["consts"], 1)
            pool.memset(TU[:, :], 1.0).then_inc(S["consts"], 1)
            pool.memset(mhalf[:, :], -0.5).then_inc(S["consts"], 1)
            pool.wait_ge(S["consts"], 3)
            pool.affine_select(out=ident[:, :], in_=ident[:, :], compare_op=ALU.not_equal, fill=1.0, base=0,
                               pattern=[[-1, P]], channel_multiplier=1).then_inc(S["consts"], 1)
            pool.affine_select(out=tri, in_=tri, compare_op=ALU.is_ge, fill=0.0, base=0,
                               pattern=[[1, P]], channel_multiplier=-1).then_inc(S["consts"], 1)

            def iota(dst, pattern, base_, cm):
                pool.iota(dst, pattern, base=base_, channel_multiplier=cm,
                          allow_small_or_imprecise_dtypes=True).then_inc(S["consts"], 1)

            iota(slot1[:, :], [[1, P]], 1, 0)
            pool.memset(eye4[:, :], 0.0).then_inc(S["eye_ready"], 1)
            for n in range(4):
                pool.wait_ge(S["eye_ready"], n + 1)
                pool.affine_select(out=eye4[:, :], in_=eye4[:, :], compare_op=ALU.not_equal, fill=1.0, base=-n * E,
                                   pattern=[[-1, E]], channel_multiplier=1).then_inc(S["eye_ready"], 1)
            iota(eid[:, :], [[1, E]], 0, 0)
            iota(tok0[:, :], [[P, NT]], -SEQ, 1)
            iota(jt[:, :], [[1, 16]], 0, 0)
            iota(jb[:, :], [[P, 16]], P, 0)
            iota(itemf[:, :], [[1, 48]], 0, 0)

            pool.memset(dup[:, :, :], 0.0).then_inc(S["dup_ready"], 1)
            for n, (first, size) in enumerate(((0, HALF), (HALF, QUARTER))):
                pool.wait_ge(S["dup_ready"], n + 1)
                pool.affine_select(out=dup[:, n, :], in_=dup[:, n, :], compare_op=ALU.not_equal, fill=1.0, base=-first,
                                   pattern=[[0, P // size], [-1, size]], channel_multiplier=1)\
                    .then_inc(S["dup_ready"], 1)

            def power(s, j):
                pool.wait_ge(S["ms_ready"], POW.index((s, j)) + 1)
                pool.tensor_tensor(rstd[:, s, j:j + 1], ms[:, s, j:j + 1], mhalf[:, j:j + 1],
                                   ALU.pow).then_inc(S["rstd_ready"], 1)

            for s_, j in POW[:NT]:
                power(s_, j)
            for n in range(32):
                qb = n % NT
                pool.wait_ge(S["l_ready"], n + 1)
                diag = L[:, n % 2, qb * P:(qb + 1) * P]
                pool.affine_select(out=diag, in_=diag, compare_op=ALU.is_ge, fill=F32_MIN, base=0,
                                   pattern=[[-1, P]], channel_multiplier=1).then_inc(S["l_masked"], 1)
                if n == LN_AT:
                    for j in range(NT):
                        power(1, j)
            for s_, j in YH:
                power(s_, j)
                if (s_, j) in ((3, NT - 1), (4, 1)):
                    n = 1 if s_ == 3 else 2
                    rows = slice(0, (3 - n) * E)
                    pool.wait_ge(S["bias_part"], n)
                    pool.tensor_tensor(bias_raw[rows, :], bias_raw[rows, :], bias3[rows, :], ALU.subtract)\
                        .then_inc(S["bias_rest"], 1)

            pool.memset(xg, 0.0).then_inc(S["xg_clear"], 1)
            bound = pool.alloc_register("bound")
            pool.reg_mov(bound, 0)

            def gather(n):
                pool.wait_ge(S["gidx_ready"], n)
                pool.reg_alu(bound, bound, SEQ - 1, ALU.max)
                pool.reg_alu(bound, bound, SEQ - 1, ALU.min)
                pool.indirect_dma_start(xg, None, token_rows, bass.IndirectOffsetOnAxis(gidx, 0),
                                        bounds_check=bound, oob_is_err=False).then_inc(S["gathered"], 16)

            def scatter(i, first=False):
                pool.wait_ge(S["ys_ready"], i + 2)
                if not first:
                    pool.wait_ge(S["cur_ready"], i + 1)
                pool.reg_alu(bound, bound, 2 * SEQ - 1, ALU.max)
                pool.reg_alu(bound, bound, 2 * SEQ - 1, ALU.min)
                for c, done in enumerate(("scattered_a", "scattered_b")):
                    pool.indirect_dma_start(sums, bass.IndirectOffsetOnAxis(scur[:, c:c + 1], 0), ys[:, c, :],
                                            None, bounds_check=bound, oob_is_err=False, compute_op=ALU.add)\
                        .then_inc(S[done], 16)
                pool.reg_alu(bound, bound, 4 * SEQ - 1, ALU.max)
                pool.indirect_dma_start(sums_q, bass.IndirectOffsetOnAxis(scur[:, 2:3], 0), ys[:, 1, 0:D // 4],
                                        None, bounds_check=bound, oob_is_err=False, compute_op=ALU.add)\
                    .then_inc(S["scattered_c"], 16)

            for j in range(NT):
                pool.wait_ge(xs_stored[j], 16)
            pool.wait_ge(S["xg_clear"], 1)
            gather(1)
            pool.wait_ge(S["h_stored"], 16)
            scatter(-1, first=True)

            def item(i):
                gather(i + 2)
                scatter(i)

            with pool.Fori(0, E) as i:
                item(i)
            nov = pool.value_load(nov_i[0:1, 0:1], min_val=0, max_val=EXTRA)
            with pool.Fori(0, EXTRA) as j:
                with pool.If(j < nov):
                    item(j + E)
            for s_, j in TAIL:
                power(s_, j)

        @block.scalar
        def _(act):
            def row(v):
                return v.rearrange("(r n) -> r n", n=P)

            for r, v in ((V_MIX, row(g_mix[0])), (V_A, row(g_a[0])), (V_B, row(g_b[0])), (V_MOE, row(g_moe[0])),
                         (V_PLE, row(g_ple[0])), (V_BS, b_s[0])):
                act.dma_start(vec_nat[r:r + v.shape[0], :], v).then_inc(S["vec_in"], 16)

            def square(src, s, j, to):
                n = SQ.index((s, j))
                if n >= 2:
                    act.wait_ge(S["sq_ready"], n - 1 if s < 5 else n)
                act.activation(to, src, ACT.Square, accum_out=ss[:, s, j:j + 1]).then_inc(S["sq_ready"], 1)

            for j in range(NT):
                act.wait_ge(x_in[j], 16)
                square(h[:, j, :].rearrange("p (a n) -> p a n", a=2), 0, j,
                       VV[:, 0, 2 * (j % 2):2 * (j % 2) + 2, :])
            act.dma_start(wr[:, :, :], w_router[0].rearrange("(k p) n -> p k n", p=P)).then_inc(S["wr_in"], 16)
            act.dma_start(bfb[:, :], row_bc(b_f)).then_inc(S["bc_in"], 16)
            act.dma_start(brb[:, :], row_bc(b_router)).then_inc(S["bc_in"], 16)

            act.wait_ge(S["fl_ready"], 2)
            act.activation(fabs[:, :, :], fabs[:, :, :], ACT.Exp).then_inc(S["fexp_ready"], 1)
            act.wait_ge(S["fexp_ready"], 1)
            act.activation(fln[:, :, :], fabs[:, :, :], ACT.Ln, bias=1.0).then_inc(S["fln_ready"], 1)

            def evac(u, dst, func, scale=1.0):
                act.wait_ge(S["unit_done"], u + 1)
                act.activation(dst, bank(4 + u % 2), func, scale=scale).then_inc(S["unit_evac"], 1)

            for j in range(NT):
                evac(j, VT[:, j, :], ACT.Copy)

            def cb_evac(hh):
                act.wait_ge(S["cb_done"], hh + 1)
                if hh >= 2:
                    act.wait_ge(S["l_ready"], 4 * (hh - 1))
                act.activation(Cb[:, hh % 2, :], SM6, ACT.Copy).then_inc(S["cb_ready"], 1)

            def fill_evac(kind, j):
                u = fill_unit(kind, j)
                if kind == "q":
                    if j >= 2:
                        act.wait_ge(S["s_done"], 8 * (j - 1))
                    evac(u, QK[:, 0, j % 2, :], ACT.Copy, scale=HD ** -0.5)
                elif kind == "k":
                    evac(u, QK[:, 1, j % 2, :], ACT.Copy)
                else:
                    evac(u, VA[:, j, :] if kind == "va" else YC[:, j, 0:512], ACT.Copy)

            def gelu(t, tiles, done):
                act.wait_ge(S["unit_evac"], fill_unit(*FILL[7 if done is S["va_gelu"] else 12]) + 1)
                for j in tiles:
                    act.activation(t(j), t(j), ACT.Gelu).then_inc(done, 1)

            def softmax_exp(n):
                w = (n % NT + 1) * P
                act.wait_ge(S["max_ready"], n + 1)
                if n >= 2:
                    act.wait_ge(S["pt_done"], n - 1)
                act.activation(Pr[:, n % 2, 0:w], L[:, n % 2, 0:w], ACT.Exp, bias=nmax[:, n:n + 1],
                               accum_out=psumr[:, n:n + 1]).then_inc(S["p_ready"], 1)

            def pt_evac(n):
                w = (n % NT + 1) * P
                act.wait_ge(S["pt_done"], n + 1)
                if n >= 2:
                    act.wait_ge(S["pv_done"], n - 1)
                act.activation(PT[:, n % 2, 0:w], bank(2 + n % 2)[:, 0:w], ACT.Copy).then_inc(S["pt_odd"], 1)

            evac(4, QK[:, 0, 0, :], ACT.Copy, scale=HD ** -0.5)
            evac(5, QK[:, 1, 0, :], ACT.Copy)
            cb_evac(0)
            for n in range(33):
                if n % 4 == 1 and n // 4 + 1 < NH:
                    cb_evac(n // 4 + 1)
                for kind, j in filled_before(n):
                    if (kind, j) != FILL[-1]:
                        fill_evac(kind, j)
                if n == LN_AT - 2:
                    gelu(lambda j: VA[:, j, :], range(NT), S["va_gelu"])
                if n < 32:
                    softmax_exp(n)
                if n >= 1 and (n - 1) % 2:
                    pt_evac(n - 1)
            gelu(lambda j: YC[:, j, 0:512], range(NT - 1), S["u_gelu"])
            evac(N_PROJ - 1, YC[:, NT - 1, 0:512], ACT.Gelu)
            act.wait_ge(S["sgu_evac"], NG)
            act.wait_ge(S["y_ready"], 32)
            for j in range(NT):
                square(YC[:, j, 0:512], 2, j, L[:, 0, :])
                square(YC[:, j, 512:1024], 3, j, L[:, 1, :])

            def bias_cast(n):
                rows = slice(0, (3 - n) * E)
                if n:
                    act.wait_ge(S["bias_rest"], n)
                act.activation(bias3[rows, :], bias_raw[rows, :], ACT.Copy).then_inc(S["bias_part"], 1)

            act.wait_ge(S["bias_in"], 6 * 16)
            bias_cast(0)
            for j in range(NT):
                act.wait_ge(S["h_ready"], 2 * j + 2)
                square(h[:, j, :], 4, j, scr[:, 0:1024] if j % 2 else scr[:, 1024:2048])
                if j in (0, 2):
                    bias_cast(j // 2 + 1)
                if j >= 1:
                    act.wait_ge(S["xs_ready"], 2 * NT + j)
                    act.dma_start(rows_v[:, j - 1, :], XS[:, (j - 1) % 2, :]).then_inc(xs_stored[j - 1], 16)
            def ple_evac(u):
                act.wait_ge(S["pw_done"], u + 1)
                act.activation(PW[:, u // 2, (u % 2) * 512:(u % 2) * 512 + 512], ple_bank(u), ACT.Copy)\
                   .then_inc(S["pw_evac"], 1)

            ple_evac(0)
            ple_evac(1)
            act.wait_ge(S["xs_ready"], 3 * NT)
            act.dma_start(rows_v[:, NT - 1, :], XS[:, (NT - 1) % 2, :]).then_inc(xs_stored[-1], 16)
            act.dma_start(sums_v, h[:, :, :]).then_inc(S["h_stored"], 16)
            for u in range(2, 5):
                ple_evac(u)
            act.wait_ge(S["route_step"], step("shift"))
            act.activation(gate4[:, :, :], gate4[:, :, :], ACT.Exp).then_inc(S["gexp_ready"], 1)
            for u in range(5, 8):
                ple_evac(u)
            def item(i):
                for c in range(2):
                    act.wait_ge(S["g_ready"], i * 2 + (c + 1))
                    act.activation(sbuf[:, c, :], gbuf[:, c, :], ACT.Sigmoid, scale=ALPHA).then_inc(S["sig_ready"], 1)
                for c in range(2):
                    act.wait_ge(S["atrans_done"], i * 2 + (c + 1))
                    act.activation(XT[:, 6 + c, :], bank(c), ACT.Copy).then_inc(S["at_ready"], 1)
                act.wait_ge(S["chunk_used"], (i + 1) * NCHUNK)
                act.wait_ge(S["cur_ready"], i + 1)
                act.wait_ge(S["scattered_a"], (i + 1) * 16)
                act.wait_ge(S["scattered_b"], (i + 1) * 16)
                act.wait_ge(S["scattered_c"], (i + 1) * 16)
                act.activation(ys[:, 0, :], bank(6), ACT.Copy, scale=gcur[:, 0, :])
                act.activation(ys[:, 1, :], bank(7), ACT.Copy, scale=gcur[:, 1, :]).then_inc(S["ys_ready"], 1)

            with act.Fori(0, E) as i:
                item(i)
            nov = act.value_load(nov_i[0:1, 0:1], min_val=0, max_val=EXTRA)
            with act.Fori(0, EXTRA) as j:
                with act.If(j < nov):
                    item(j + E)

            def tail_square(s, j):
                if s == 5:
                    act.wait_ge(sum_in[j], 16)
                else:
                    act.wait_ge(S["ple_ready"], 2 * j + 2)
                square(h[:, j, :], s, j, junk)

            def gate_sigmoids(j):
                for c in range(2):
                    k = 2 * j + c
                    act.wait_ge(S["unit_done"], 32 + k + 1)
                    if k >= 2:
                        act.wait_ge(S["ple_ready"], k - 1)
                    act.activation(sg[:, c, :], bank(4 + c), ACT.Sigmoid).then_inc(S["sg_ready"], 1)

            for j in range(NT):
                tail_square(5, j)
            for j in range(NT):
                gate_sigmoids(j)
                tail_square(6, j)

        @block.tensor
        def _(pe):
            def mm(dst, lhsT, rhs, start, stop, shared=False):
                return pe.matmul(dst, lhsT, rhs, start=start, stop=stop, skip_group_check=shared)

            def transpose_tile(n):
                pe.wait_ge(S["xs_ready"], n + 1)
                if n >= 2:
                    pe.wait_ge(S["tp_evac"], n - 1)
                for k in range(KD):
                    last = pe.transpose(PAIR[n % 2][:, k, :], XS[:, n % 2, k * P:(k + 1) * P], ident[:, :])
                last.then_inc(S["tp_done"], 1)

            pe.wait_ge(S["consts"], 5)
            pe.wait_ge(S["vec_in"], 96)
            pe.transpose(SM6[:, 0:36], vec_nat, ident[0:36, 0:36]).then_inc(S["vecT_done"], 1)
            for j in range(NT):
                transpose_tile(j)
            pe.wait_ge(S["tp_evac"], NT)
            pe.wait_ge(S["ws_in"], 16)
            for g in range(NG):
                last = pe.transpose(bank(2)[:, g * P:(g + 1) * P], ws_nat[:, g, :], ident[:, :])
            last.then_inc(S["ws_done"], 1)
            def narrow(w, n, part_done, part_ready, dst, done):
                for k in range(KD):
                    lo = (k % 4) * E
                    last = mm(SM7[lo:lo + n, :], w[:, k, :], XT[:, k, :], k < 4, k >= 4, True)
                last.then_inc(part_done, 1)
                pe.wait_ge(part_ready, 1)
                for j in range(NT):
                    last = mm(dst[:, j, :], quarters[:, j * P:(j + 1) * P], eye4[:, 0:n], True, True)
                last.then_inc(done, 1)

            pe.wait_ge(S["wf_in"], 16)
            pe.wait_ge(S["zero7"], 1)
            pe.wait_ge(S["eye_ready"], 5)
            narrow(wf, NH, S["fpart_done"], S["fpart_ready"], f_ps, S["f_done"])

            def free_unit(u):
                if 2 <= u < N_PROJ + 2:
                    pe.wait_ge(S["unit_evac"], u - 1)
                elif N_PROJ + 2 <= u < N_SGU + 2:
                    pe.wait_ge(S["sgu_evac"], u - N_PROJ - 1)
                elif N_SGU + 2 <= u < 32:
                    pe.wait_ge(S["h_ready"], u - N_SGU - 1)
                elif u >= 34:
                    pe.wait_ge(S["sg_ready"], u - 33)

            def unit(u, lhsT, rhs, nk=KD, ks=None):
                ks = range(nk) if ks is None else ks
                if ks[0] == 0:
                    free_unit(u)
                for k in ks:
                    last = mm(bank(4 + u % 2), lhsT(k), rhs(k), k == 0, k == nk - 1)
                if ks[-1] == nk - 1:
                    last.then_inc(S["unit_done"], 1)

            def tile_of(j):
                return lambda k: XT[:, k, j * P:(j + 1) * P]

            def cols_of(w, c=None):
                return lambda k: w[:, k, :] if c is None else w[:, k, c * P:(c + 1) * P]

            def all_tokens(k):
                return XT[:, k, :]

            pe.wait_ge(blk_in["v"], 16)
            unit(0, tile_of(0), cols_of(W_V))
            unit(1, tile_of(1), cols_of(W_V))
            pe.wait_ge(S["logf_ready"], 1)
            for j in range(NT):
                for i in range(j + 1):
                    last = mm(c_ps[:, j, :], tri if i == j else ones, logf[:, i, :], i == 0, i == j)
            last.then_inc(S["c_done"], 1)
            for j in range(2, NT):
                unit(j, tile_of(j), cols_of(W_V))
            pe.wait_ge(blk_in["q"], 16)
            unit(4, cols_of(W_Q, 0), all_tokens)
            pe.wait_ge(blk_in["k"], 16)
            unit(5, cols_of(W_K, 0), all_tokens)

            def forget_rows(hh):
                if hh:
                    pe.wait_ge(S["cb_ready"], hh)
                for j in range(NT):
                    last = mm(SM6[:, j * P:SEQ], logf[:, j, hh:hh + 1].to_broadcast([P, P]),
                              TU[:, 0:SEQ - j * P], j == 0, j == NT - 1, True)
                last.then_inc(S["cb_done"], 1)

            def scores(n):
                hh, qb = divmod(n, NT)
                pair, r = divmod(hh, 2)
                if n % 8 == 0:
                    pe.wait_ge(S["unit_evac"], fill_unit("k", pair) + 1 if pair else 6)
                if n >= 2:
                    pe.wait_ge(S["l_ready"], n - 1)
                mm(bank(n % 2)[:, 0:(qb + 1) * P], QK[r * HD:(r + 1) * HD, 0, pair % 2, qb * P:(qb + 1) * P],
                   QK[r * HD:(r + 1) * HD, 1, pair % 2, 0:(qb + 1) * P], True, True).then_inc(S["s_done"], 1)

            def transpose_probs(n):
                pe.wait_ge(S["p_ready"], n + 1)
                if n >= 2:
                    pe.wait_ge(S["pt_odd" if n % 2 else "pt_even"], n // 2)
                for b in range(n % NT + 1):
                    last = pe.transpose(bank(2 + n % 2)[:, b * P:(b + 1) * P], Pr[:, n % 2, b * P:(b + 1) * P],
                                        ident[:, :])
                last.then_inc(S["pt_done"], 1)

            def values(n):
                hh, qb = divmod(n, NT)
                pe.wait_ge(S["pt_odd" if n % 2 else "pt_even"], n // 2 + 1)
                if n:
                    pe.wait_ge(S["y_ready"], n)
                for b in range(qb + 1):
                    last = mm(o_ps, PT[:, n % 2, b * P:(b + 1) * P], VT[:, b, hh * HD:(hh + 1) * HD],
                              b == 0, b == qb)
                last.then_inc(S["pv_done"], 1)

            pe.wait_ge(S["ctok_ready"], 1)
            pe.wait_ge(S["ws_evac"], 1)
            forget_rows(0)

            def fill(n):
                for i in fill_of(n):
                    kind, j = FILL[i // KD]
                    if i % KD == 0 and j == (1 if kind in "qk" else 0):
                        pe.wait_ge(blk_in[kind], 16)
                    w = {"q": W_Q, "k": W_K, "va": W_VA, "u": W_U}[kind]
                    if kind in ("q", "k"):
                        unit(fill_unit(kind, j), cols_of(w, j), all_tokens, ks=[i % KD])
                    else:
                        unit(fill_unit(kind, j), tile_of(j), cols_of(w), ks=[i % KD])

            for n in range(34):
                if n % 4 == 1 and n // 4 + 1 < NH:
                    forget_rows(n // 4 + 1)
                if n < 32:
                    scores(n)
                    fill(n)
                if 1 <= n <= 32:
                    transpose_probs(n - 1)
                if n >= 2:
                    values(n - 2)
            pe.wait_ge(S["va_ready"], NT)
            for g in range(NG):
                unit(N_PROJ + g, lambda k: wsT[:, g, :], lambda k: VA[:, :, g * P:(g + 1) * P], nk=1)

            def out_projection(j):
                pe.wait_ge(S["tp_evac"], NT + j + 1)
                if j == 0:
                    pe.wait_ge(blk_in["oa"], 16)
                    pe.wait_ge(blk_in["ob"], 16)
                unit(N_SGU + 2 * j, tile_of(j), cols_of(W_OA))
                unit(N_SGU + 2 * j + 1, tile_of(j), cols_of(W_OB))

            transpose_tile(4)
            transpose_tile(5)
            out_projection(0)
            transpose_tile(6)
            out_projection(1)
            transpose_tile(7)
            out_projection(2)
            transpose_tile(8)
            pe.wait_ge(S["p_in"], 16)
            pe.wait_ge(S["cb_ready"], NH)
            for k in range(2):
                for j in range(NT):
                    last = pe.transpose(bank(6 + k)[:, j * P:(j + 1) * P], pnat[:, j, k * P:(k + 1) * P], ident[:, :])
            last.then_inc(S["pT_done"], 1)
            out_projection(3)

            def ple_product(u):
                j, c = divmod(u, 2)
                if u >= 2:
                    pe.wait_ge(S["pw_evac"], u - 1)
                for k in range(2):
                    last = mm(ple_bank(u), pT[:, k, j * P:(j + 1) * P], wple_sb[:, k, c * 512:(c + 1) * 512],
                              k == 0, k == 1)
                last.then_inc(S["pw_done"], 1)

            transpose_tile(9)
            pe.wait_ge(S["pT_ready"], 1)
            pe.wait_ge(S["wple_in"], 16)
            for n, us in ((10, (0, 1)), (11, (2, 3, 4))):
                for u in us:
                    ple_product(u)
                transpose_tile(n)
            pe.wait_ge(S["tp_evac"], 12)
            pe.wait_ge(S["pw_evac"], 5)
            pe.wait_ge(S["wr_in"], 16)
            narrow(wr, E, S["lpart_done"], S["lpart_ready"], lg_ps, S["lg_done"])
            ple_product(5)
            ple_product(6)
            pe.wait_ge(S["route_step"], step("mk"))
            for j in range(NT):
                for i in range(j + 1):
                    mm(rank_ps[:, j, :], tri if i == j else ones, Mk[:, i, :], i == 0, i == j)
            for j in range(NT):
                last = mm(cnt_ps, ones, Mk[:, j, :], j == 0, j == NT - 1)
            last.then_inc(S["rank_done"], 1)

            def list_tokens(n):
                pe.wait_ge(S["sel_ready"], n)
                for j in range(NT):
                    last = mm(idx_ps, selm[:, j, :], dcur[:, j, :], j == 0, j == NT - 1)
                last.then_inc(S["idxmm_done"], 1)

            def transpose_rows(n, item_before=True):
                pe.wait_ge(S["gathered"], n * 16)
                pe.wait_ge(S["list_ready"], n)
                if item_before:
                    pe.wait_ge(S["cur_ready"], n - 1)
                for k in range(KD):
                    last = pe.transpose(T_ps[:, k, :], xg[:, k * P:(k + 1) * P], ident[:, :])
                last.then_inc(S["xtrans_done"], 1)

            list_tokens(1)
            pe.wait_ge(S["route_step"], step("cnt"))
            for j in range(NT):
                last = mm(cntT_ps, Mk[:, j, :], ones[:, 0:1], j == 0, j == NT - 1)
            last.then_inc(S["cnt_done"], 1)
            pe.wait_ge(S["route_step"], step("ext3"))
            mm(xin_ps, extT[:, 2:3].to_broadcast([E, P]), TU[0:E, 0:E], True, True).then_inc(S["xin_done"], 1)
            ple_product(7)
            transpose_rows(1, item_before=False)

            def gate_up(k, part, lo, n):
                return ring[:, k, part * F + lo:part * F + lo + n]

            def gu_bias(part, lo, n):
                return bias3[:, part * F + lo:part * F + lo + n]

            def down(f, lo, n):
                at = (f % 2) * D + lo
                return ring[:, 8 + f // 2, at:at + n]

            def dn_bias(lo, n):
                return bias3[:, 2 * F + lo:2 * F + lo + n]

            def tiles(size):
                return [(slice(g * size, (g + 1) * size), g * (D * size // P)) for g in range(P // size)]

            def halves(b, lhsT, rhs, start, stop):
                for rows, lo in tiles(HALF):
                    last = mm(bank(b)[rows, :], lhsT, rhs(lo, D // 2), start, stop, True)
                return last

            def quarters_of(b, lhsT, rhs, start, stop):
                for rows, lo in tiles(QUARTER):
                    last = mm(bank(b)[rows, 0:D // 4], lhsT, rhs(lo, D // 4), start, stop, True)
                return last

            def product(kind, b, c, lhsT, rhs, start, stop):
                if kind == LARGE:
                    return mm(bank(b), lhsT, rhs(c * 512, 512), start, stop, True)
                if c == 0:
                    return halves(b, lhsT[:, 0:HALF], rhs, start, stop)
                return quarters_of(b, lhsT[:, HALF:HALF + QUARTER], rhs, start, stop)

            def item(i, kind):
                parts = range(1 if kind == SMALL else 2)
                pe.wait_ge(S["xt_ready"], i + 1)
                pe.wait_ge(S["list_ready"], i + 1)
                for n in range(2):
                    last = mm(dup_ps[:, n, :], ident[:, :] if kind == LARGE else dup[:, n, :], lcur, True, True)
                last.then_inc(S["dup_done"], 1)
                pe.wait_ge(S["at_ready"], i * 2 + 1)
                pe.wait_ge(S["act_ready"], i * 2 + 1)
                pieces = [(part, c) for part in range(2) for c in parts]
                for k in range(KD):
                    pe.wait_ge(arrived[k], (i + 1) * 16)
                    for n, (part, c) in enumerate(pieces):
                        last = product(kind, 2 * c + part, c, xTm[:, k, :],
                                       lambda lo, m: gate_up(k, part, lo, m), k == 0, k == KD - 1)
                        if k == KD - 1 and n < len(pieces) - 1:
                            last.then_inc(S["gu_done"], 2 if kind == SMALL else 1)
                    last.then_inc(S["chunk_used"], 1)
                    if k == 1:
                        list_tokens(i + 2)
                        pe.wait_ge(S["esel_ready"], i + 1)
                        for part, c in pieces:
                            product(kind, 2 * c + part, c, esel[:, :], lambda lo, m: gu_bias(part, lo, m), False, False)
                pe.wait_ge(S["ys_ready"], i + 1)
                for c in parts:
                    last = product(kind, 6 + c, c, esel[:, :], dn_bias, True, False)
                if kind == SMALL:
                    last.then_inc(S["gu_done"], 1)

                def transpose_activations(c):
                    pe.wait_ge(S["act_ready"], i * 2 + (c + 2))
                    for f in range(2 if kind == MEDIUM and c else 4):
                        last = pe.transpose(bank(c)[:, f * P:(f + 1) * P], ubuf[:, c, f * P:(f + 1) * P], ident[:, :])
                    last.then_inc(S["atrans_done"], 2 if kind == SMALL else 1)

                def down_product(f, c):
                    if kind == LARGE:
                        lhsT = aT[:, f, :]
                    elif c == 0:
                        lhsT = aT[:, f % 4, (f // 4) * HALF:(f // 4 + 1) * HALF]
                    else:
                        lhsT = aT[:, 4 + f % 2, (f // 2) * QUARTER:(f // 2 + 1) * QUARTER]
                    rhs = lambda lo, m: down(f, lo, m)
                    if kind == LARGE:
                        return mm(bank(6 + c), lhsT, rhs(c * 512, 512), False, f == KD - 1, True)
                    return (quarters_of if c else halves)(6 + c, lhsT, rhs, False, f == KD - 1)

                transpose_activations(0)
                transpose_rows(i + 2)
                behind = 4 if kind == MEDIUM else 0
                for f in range(KD):
                    if f % 2 == 0:
                        pe.wait_ge(arrived[8 + f // 2], (i + 1) * 16)
                    if f in (0, 4):
                        pe.wait_ge(S["at_ready"], i * 2 + (2 if kind == SMALL or f == 0 else 3))
                    if f == 2 and kind != SMALL:
                        transpose_activations(1)
                    if behind and f == behind:
                        for g in range(behind):
                            last = down_product(g, 1)
                            if g % 2:
                                last.then_inc(S["chunk_used"], 1)
                    for c in parts:
                        if c == 0 or f >= behind:
                            last = down_product(f, c)
                    if f % 2 and f >= behind:
                        last.then_inc(S["chunk_used"], 1)

            pe.wait_ge(S["pw_evac"], 8)
            pe.wait_ge(S["bias_part"], 3)
            with pe.Fori(0, E) as i:
                kind = pe.value_load(kind_i[0:1, bass.ds(i, 1)], min_val=0, max_val=SMALL)
                with pe.If(kind > MEDIUM):
                    item(i, SMALL)
                with pe.Else():
                    with pe.If(kind > LARGE):
                        item(i, MEDIUM)
                    with pe.Else():
                        item(i, LARGE)
            pe.wait_ge(S["route_step"], step("nov_i"))
            nov = pe.value_load(nov_i[0:1, 0:1], min_val=0, max_val=EXTRA)
            with pe.Fori(0, EXTRA) as j:
                with pe.If(j < nov):
                    item(j + E, LARGE)
            pe.wait_ge(S["wpg_in"], 16)
            transpose_tile(12)
            for j in range(NT):
                if j + 1 < NT:
                    transpose_tile(12 + j + 1)
                pe.wait_ge(S["tp_evac"], 12 + j + 1)
                for c in range(2):
                    unit(32 + 2 * j + c, tile_of(j), lambda k: wpg_sb[:, k, c * 512:(c + 1) * 512])

        @block.vector
        def _(dve):
            ts, tt, stt = dve.tensor_scalar, dve.tensor_tensor, dve.scalar_tensor_tensor

            def mean_square(s, j, n):
                dve.wait_ge(S["sq_ready"], SQ.index((s, j)) + 1)
                ts(ms[:, s, j:j + 1], ss[:, s, j:j + 1], 1.0 / n, RMS_EPS, ALU.mult, ALU.add)\
                    .then_inc(S["ms_ready"], 1)

            def rstd_of(s, j):
                dve.wait_ge(S["rstd_ready"], POW.index((s, j)) + 1)
                return rstd[:, s, j:j + 1]

            def normalise(n, pieces):
                scales = [(lo, src, rstd_of(s, j)) for lo, src, s, j in pieces]
                if n >= 2:
                    dve.wait_ge(S["tp_done"], n - 1)
                if n in (10, 11):
                    dve.wait_ge(xs_stored[n - 10], 16)
                for lo, src, r in scales:
                    last = ts(XS[:, n % 2, lo:lo + src.shape[1]], src, r, None, ALU.mult)
                last.then_inc(S["xs_ready"], 1)

            def take_transposed(n, v):
                j = n % NT
                dve.wait_ge(S["tp_done"], n + 1)
                tt(XT[:, :, j * P:(j + 1) * P], PAIR[n % 2], spread(vecT[:, v:v + KD], P),
                   ALU.mult).then_inc(S["tp_evac"], 1)

            for lo, hi, m, values in [(0, P, LARGE, (2 * SEQ, 2 * SEQ + 1, OOB))] + [
                    (lo, lo + HALF, m, (2 * SEQ + lo // HALF, OOB)) for m in (MEDIUM, SMALL) for lo in (0, HALF)]:
                for c, value in enumerate(values):
                    dve.memset(offs[lo:hi, m, c:c + 1], float(value)).then_inc(S["offs_ready"], 1)
            dve.memset(offs[:, SMALL, 2:3], float(OOB)).then_inc(S["offs_ready"], 1)
            for g in range(4):
                dve.memset(offs[g * QUARTER:(g + 1) * QUARTER, MEDIUM, 2:3], 4.0 * SEQ + g).then_inc(S["offs_ready"], 1)
            dve.memset(SM7, 0.0).then_inc(S["zero7"], 1)
            dve.wait_ge(S["vecT_done"], 1)
            dve.tensor_copy(vecT[:, :], SM6[:, 0:36]).then_inc(S["vecT_ready"], 1)
            dve.wait_ge(S["vecT_ready"], 1)

            def x_scale(j):
                mean_square(0, j, D)
                normalise(j, [(0, h[:, j, :], 0, j)])

            x_scale(0)
            x_scale(1)
            for j in range(NT):
                take_transposed(j, V_MIX)
                if j + 2 < NT:
                    x_scale(j + 2)
            dve.wait_ge(S["ws_done"], 1)
            dve.tensor_copy(wsT[:, :, :], bank(2).rearrange("p (g i) -> p g i", g=NG)).then_inc(S["ws_evac"], 1)
            dve.wait_ge(S["ws_evac"], 1)
            dve.memset(wsT[64:P, :, 0:64], 0.0)
            dve.wait_ge(S["fpart_done"], 1)
            dve.tensor_copy(quarters, SM7).then_inc(S["fpart_ready"], 1)
            dve.wait_ge(S["f_done"], 1)
            dve.wait_ge(S["bc_in"], 32)
            tt(fl[:, :, :], f_ps, stack(bfb[:, :], NT), ALU.add)\
                .then_inc(S["fl_ready"], 1)
            dve.wait_ge(S["fl_ready"], 1)
            stt(fabs[:, :, :], fl[:, :, :], -1.0, fl[:, :, :], ALU.mult, ALU.min).then_inc(S["fl_ready"], 1)
            dve.wait_ge(S["fln_ready"], 1)
            stt(logf[:, :, :], fl[:, :, :], 0.0, fln[:, :, :], ALU.min, ALU.subtract).then_inc(S["logf_ready"], 1)
            dve.wait_ge(S["c_done"], 1)
            dve.tensor_copy(ctok[:, :, :], c_ps).then_inc(S["ctok_ready"], 1)

            def ln_statistics():
                dve.wait_ge(S["va_gelu"], NT)
                for j in range(NT):
                    dve.bn_stats(lnst[:, j, :], VA[:, j, :]).then_inc(S["ln_stat"], 1)
                dve.wait_ge(S["ln_stat"], NT)
                for j in range(NT):
                    dve.bn_aggr(lnmv[:, j, :], lnst[:, j, :]).then_inc(S["ln_var"], 1)
                dve.wait_ge(S["ln_var"], NT)
                for j in range(NT):
                    ts(ms[:, 1, j:j + 1], lnmv[:, j, 1:2], LN_EPS, None, ALU.add).then_inc(S["ms_ready"], 1)

            def ln_apply(j):
                rs = rstd_of(1, j)
                dve.wait_ge(S["ln_in"], 32)
                ts(VA[:, j, :], VA[:, j, :], lnmv[:, j, 0:1], rs, ALU.subtract, ALU.mult).then_inc(S["ln_step"], 1)
                dve.wait_ge(S["ln_step"], 2 * j + 1)
                tt(VA[:, j, :], VA[:, j, :], lng, ALU.mult).then_inc(S["ln_step"], 1)
                dve.wait_ge(S["ln_step"], 2 * j + 2)
                tt(VA[:, j, :], VA[:, j, :], lnb, ALU.add).then_inc(S["va_ready"], 1)

            def logits(n):
                hh, qb = divmod(n, NT)
                w = (qb + 1) * P
                dve.wait_ge(S["s_done"], n + 1)
                dve.wait_ge(S["cb_ready"], hh + 1)
                if n >= 2:
                    dve.wait_ge(S["p_ready"], n - 1)
                stt(L[:, n % 2, 0:w], bank(n % 2)[:, 0:w], ctok[:, qb, hh:hh + 1], Cb[:, hh % 2, 0:w],
                    ALU.add, ALU.subtract).then_inc(S["l_ready"], 1)

            def row_max(n):
                dve.wait_ge(S["l_masked"], n + 1)
                dve.tensor_reduce(nmax[:, n:n + 1], L[:, n % 2, 0:(n % NT + 1) * P], AX, ALU.max, negate=True)\
                    .then_inc(S["max_ready"], 1)

            def take_probs(n):
                w = (n % NT + 1) * P
                dve.wait_ge(S["pt_done"], n + 1)
                if n >= 2:
                    dve.wait_ge(S["pv_done"], n - 1)
                dve.tensor_copy(PT[:, n % 2, 0:w], bank(2 + n % 2)[:, 0:w]).then_inc(S["pt_even"], 1)

            def outputs(n):
                hh, qb = divmod(n, NT)
                dve.wait_ge(S["p_ready"], n + 1)
                dve.reciprocal(rsum[:, n:n + 1], psumr[:, n:n + 1]).then_inc(S["r_ready"], 1)
                dve.wait_ge(S["r_ready"], n + 1)
                dve.wait_ge(S["pv_done"], n + 1)
                ts(YC[:, qb, GW + hh * HD:GW + (hh + 1) * HD], o_ps, rsum[:, n:n + 1], None, ALU.mult)\
                    .then_inc(S["y_ready"], 1)

            for n in range(35):
                if n < 32:
                    logits(n)
                if 1 <= n <= 32:
                    row_max(n - 1)
                if 2 <= n < 34 and n % 2 == 0:
                    take_probs(n - 2)
                if n >= 3:
                    outputs(n - 3)
                if n == LN_AT:
                    ln_statistics()
                if LN_FROM <= n < LN_FROM + NT:
                    ln_apply(n - LN_FROM)
            dve.wait_ge(S["u_gelu"], NT - 1)
            dve.wait_ge(S["unit_evac"], N_PROJ)
            for g in range(NG):
                cols = YC[:, :, g * P:(g + 1) * P]
                dve.wait_ge(S["unit_done"], N_PROJ + g + 1)
                stt(cols, bank(4 + g % 2).rearrange("p (j c) -> p j c", j=NT), vecT[:, V_BS + g:V_BS + g + 1],
                    cols, ALU.add, ALU.mult).then_inc(S["sgu_evac"], 1)

            def y_scale(j):
                mean_square(2, j, GW)
                mean_square(3, j, FW)
                normalise(4 + j, [(0, YC[:, j, 0:GW], 2, j), (GW, YC[:, j, GW:D], 3, j)])

            def residual(j):
                for c in range(2):
                    u = N_SGU + 2 * j + c
                    dve.wait_ge(S["unit_done"], u + 1)
                    tt(h[:, j, c * 512:(c + 1) * 512], h[:, j, c * 512:(c + 1) * 512], bank(4 + c), ALU.add)\
                        .then_inc(S["h_ready"], 1)

            def h_scale(j):
                mean_square(4, j, D)
                normalise(8 + j, [(0, h[:, j, :], 4, j)])

            y_scale(0)
            y_scale(1)
            take_transposed(4, V_A)
            y_scale(2)
            take_transposed(5, V_A)
            residual(0)
            y_scale(3)
            take_transposed(6, V_A)
            residual(1)
            take_transposed(7, V_A)
            h_scale(0)
            residual(2)
            h_scale(1)
            dve.memset(scur, OOB)
            dve.memset(ys, 0.0).then_inc(S["ys_ready"], 1)
            take_transposed(8, V_MOE)
            dve.wait_ge(S["pT_done"], 1)
            dve.tensor_copy(pT, bank(6, 2).rearrange("p (k t) -> p k t", k=2)).then_inc(S["pT_ready"], 1)
            residual(3)
            h_scale(2)
            take_transposed(9, V_MOE)
            h_scale(3)
            take_transposed(10, V_MOE)
            take_transposed(11, V_MOE)

            def r(name, ins, wait=True):
                ins.then_inc(S["route_step"], 1)
                if wait:
                    dve.wait_ge(S["route_step"], step(name))

            dve.wait_ge(S["eye_ready"], 5)
            dve.tensor_copy(eye3[:, :], eye4[0:3 * E, :]).then_inc(S["offs_ready"], 1)
            dve.memset(ahead[:, 0:1], 0.0).then_inc(S["at_ready"], 1)
            dve.memset(ahead[:, 1:2], 0.0).then_inc(S["act_ready"], 1)
            dve.wait_ge(S["lpart_done"], 1)
            dve.tensor_copy(quarters, SM7).then_inc(S["lpart_ready"], 1)
            dve.wait_ge(S["lg_done"], 1)
            r("bias", tt(lg[:, :, :], lg_ps, stack(brb[:, :], NT),
                         ALU.add))
            for j in range(NT):
                r(f"max{j}", dve.max(top[:, j, :], lg[:, j, :]))
            for j in range(NT):
                r(f"arg{j}", dve.max_index(topi[:, j, :], top[:, j, :], lg[:, j, :]))
            r("argf", dve.tensor_copy(topf[:, :, :], topi[:, :, :]))
            r("shift", tt(gate4[:, :, :], top[:, :, 0:TOPK], top[:, :, 0:1].to_broadcast([P, NT, TOPK]), ALU.subtract))
            dve.wait_ge(S["gexp_ready"], 1)
            r("gsum", dve.tensor_reduce(gsum[:, :], gate4[:, :, :], AX, ALU.add))
            r("grcp", dve.reciprocal(gsum[:, :], gsum[:, :]))
            r("gates", tt(gate4[:, :, :], gate4[:, :, :],
                          spread(gsum[:, :], TOPK), ALU.mult))
            for k in range(TOPK):
                last = tt(eq[:, k], topf[:, :, k:k + 1].to_broadcast([P, NT, E]),
                          stack(eid[:, :], NT), ALU.is_equal)
            r("eq", last)
            r("mk", dve.tensor_reduce(Mk[:, :, :], eq.rearrange("p k j e -> p j e k"), AX, ALU.add))
            for k in range(TOPK):
                last = tt(wq[:, k], eq[:, k], gate4[:, :, k:k + 1].to_broadcast([P, NT, E]), ALU.mult)
            r("wgate", last)
            r("gk", dve.tensor_reduce(Gk[:, :, :], wq.rearrange("p k j e -> p j e k"), AX, ALU.add))
            r("tok", dve.tensor_copy(dcur[:, :, 0], tok0[:, :]))
            r("e_first", dve.memset(item_e[:, 0:1], 0))
            r("base0", dve.memset(base[:, 0:E], 0.0))
            r("kind0", dve.memset(kind_i[:, :], 0))
            dve.wait_ge(S["rank_done"], 1)
            r("c1", tt(R1[:, :, :], rank_ps, Mk[:, :, :], ALU.mult))
            r("cnt", dve.tensor_copy(cntB[:, :], cnt_ps))
            r("kind1", ts(at_most_half, cntB[0:1, :], float(HALF), None, ALU.is_le))
            r("kind2", stt(kind_i[:, 0:E], cntB[0:1, :], float(HALF + QUARTER), at_most_half, ALU.is_le, ALU.add))

            def block_counts():
                dve.wait_ge(S["cnt_done"], 1)
                r("ext1", ts(extT[:, 0:1], cntT_ps, float(P), None, ALU.is_gt))
                r("ext2", stt(extT[:, 1:2], cntT_ps, 2.0 * P, extT[:, 0:1], ALU.is_gt, ALU.add))
                r("ext3", stt(extT[:, 2:3], cntT_ps, 3.0 * P, extT[:, 1:2], ALU.is_gt, ALU.add))

            def item_tables():
                xrow = stack(xin[:, :], 16)
                dve.wait_ge(S["xin_done"], 1)
                r("xin", dve.tensor_copy(xin[:, :], xin_ps))
                r("cmp", tt(ovc, xrow, spread(jt[:, :], E), ALU.is_le))
                r("ecount", dve.tensor_reduce(itemf[:, E:48], ovc, AX, ALU.add))
                r("val", tt(ovv, ovc, xrow, ALU.mult))
                r("vmax", dve.tensor_reduce(ovm[:, :], ovv, AX, ALU.max))
                r("clip", ts(itemf[:, E:48], itemf[:, E:48], float(E - 1), None, ALU.min))
                r("vneg", ts(ovm[:, :], ovm[:, :], -float(P), None, ALU.mult))
                r("base1", tt(base[:, E:48], ovm[:, :], jb[:, :], ALU.add))
                r("item_e", dve.tensor_copy(item_e[:, 1:48], itemf[0:1, 1:48]))
                r("nov_i", dve.tensor_copy(nov_i[:, :], xin[0:1, E - 1:E]))

            def select(i, n):
                e = dve.value_load(item_e[0:1, bass.ds(i, 1)], min_val=0, max_val=E - 1)
                kind = dve.value_load(kind_i[0:1, bass.ds(i, 1)], min_val=0, max_val=SMALL)
                for j in range(NT):
                    ts(selm[:, j, :], slot1[:, :], base[:, bass.ds(i, 1)], R1[:, j, bass.ds(e, 1)],
                       ALU.add, ALU.is_equal)
                dve.tensor_copy(dcur[:, :, 1:2], Gk[:, :, bass.ds(e, 1)]).then_inc(S["sel_ready"], 1)
                return e, kind

            def take_tokens(n):
                dve.wait_ge(S["idxmm_done"], n)
                ts(gidx, idx_ps[:, 0:1], float(SEQ), None, ALU.add).then_inc(S["gidx_ready"], 1)
                dve.tensor_copy(lcur, idx_ps).then_inc(S["list_ready"], 1)

            def take_offsets(kind):
                dve.tensor_copy(ocur, offs[:, bass.ds(kind, 1), :].rearrange("p a t -> p (a t)"))\
                    .then_inc(S["ocur_ready"], 1)

            def take_places(i):
                dve.wait_ge(S["dup_done"], i + 1)
                dve.wait_ge(S["ocur_ready"], i + 1)
                dve.tensor_copy(gcur, dup_ps[:, :, 1:2])
                stt(scur[:, 0:2], dup_ps[:, 0, 0:1].to_broadcast([P, 2]), 2.0, ocur[:, 0:2], ALU.mult, ALU.add)
                stt(scur[:, 2:3], dup_ps[:, 1, 0:1], 4.0, ocur[:, 2:3], ALU.mult, ALU.add).then_inc(S["cur_ready"], 1)

            def take_rows(e, n):
                dve.wait_ge(S["xtrans_done"], n)
                tt(xTm, T_ps, spread(vecT[:, V_MOE:V_MOE + KD], P), ALU.mult).then_inc(S["xt_ready"], 1)
                dve.tensor_copy(esel[:, :], eye3[:, bass.ds(e, 1)].to_broadcast([3 * E, P])).then_inc(S["esel_ready"], 1)

            def item(i):
                e, kind = select(i + 1, i + 2)
                take_tokens(i + 2)
                dve.wait_ge(S["ys_ready"], i + 1)
                dve.wait_ge(S["scattered_a"], (i + 1) * 16)
                dve.wait_ge(S["scattered_b"], (i + 1) * 16)
                dve.wait_ge(S["scattered_c"], (i + 1) * 16)
                take_places(i)
                dve.wait_ge(S["cur_ready"], i + 1)
                take_offsets(kind)
                for c in range(2):
                    dve.wait_ge(S["gu_done"], i * 3 + (c + 1))
                    ts(gbuf[:, c, :], bank(2 * c), LIMIT, None, ALU.min).then_inc(S["g_ready"], 1)
                for c in range(2):
                    if c == 0:
                        dve.wait_ge(S["gu_done"], i * 3 + 3)
                    else:
                        dve.wait_ge(S["chunk_used"], i * NCHUNK + 8)
                    ts(ubuf[:, c, :], bank(2 * c + 1), LIMIT, -LIMIT, ALU.min, ALU.max).then_inc(S["u_ready"], 1)
                    dve.wait_ge(S["u_ready"], i * 2 + (c + 1))
                    stt(ubuf[:, c, :], ubuf[:, c, :], 1.0, gbuf[:, c, :], ALU.add, ALU.mult).then_inc(S["a_ready"], 1)
                    dve.wait_ge(S["a_ready"], i * 2 + (c + 1))
                    dve.wait_ge(S["sig_ready"], i * 2 + (c + 1))
                    tt(ubuf[:, c, :], ubuf[:, c, :], sbuf[:, c, :], ALU.mult).then_inc(S["act_ready"], 1)
                take_rows(e, i + 2)

            dve.wait_ge(S["offs_ready"], 17)
            dve.wait_ge(S["dup_ready"], 3)
            e, kind = select(0, 1)
            take_offsets(kind)
            take_tokens(1)
            block_counts()
            take_rows(e, 1)
            item_tables()
            with dve.Fori(0, E) as i:
                item(i)
            nov = dve.value_load(nov_i[0:1, 0:1], min_val=0, max_val=EXTRA)
            with dve.Fori(0, EXTRA) as j:
                with dve.If(j < nov):
                    item(j + E)

            def add_ple(j):
                for c in range(2):
                    k, cols = 2 * j + c, slice(c * 512, (c + 1) * 512)
                    dve.wait_ge(S["sg_ready"], k + 1)
                    tt(sg[:, c, :], sg[:, c, :], PW[:, j, cols], ALU.mult).then_inc(S["ple_step"], 1)
                    dve.wait_ge(S["ple_step"], k + 1)
                    tt(h[:, j, cols], h[:, j, cols], sg[:, c, :], ALU.add).then_inc(S["ple_ready"], 1)

            def final(j):
                sc = rstd_of(6, j)
                dve.wait_ge(S["gfin_in"], 16)
                if j >= 2:
                    dve.wait_ge(out_stored[j - 2], 16)
                stt(obuf[:, j % 2, :], h[:, j, :], sc, gfin, ALU.mult, ALU.mult).then_inc(S["out_ready"], 1)

            def ple_normalise(j):
                normalise(12 + j, [(0, h[:, j, :], 5, j)])

            mean_square(5, 0, D)
            ple_normalise(0)
            mean_square(5, 1, D)
            ple_normalise(1)
            take_transposed(12, V_PLE)
            mean_square(5, 2, D)
            ple_normalise(2)
            mean_square(5, 3, D)
            take_transposed(13, V_PLE)
            ple_normalise(3)
            for j in range(NT):
                if j + 2 < NT:
                    take_transposed(12 + j + 2, V_PLE)
                add_ple(j)
                mean_square(6, j, D)
                final(j)


_INS = ["x", "p", "g_mix", "w_in", "ln_g", "ln_b", "w_s", "b_s", "b_f", "g_a", "g_b", "w_out", "g_moe", "w_router",
        "b_router", "w_gu", "b_gu", "w_dn", "b_dn", "g_ple", "w_ple_gate", "w_ple", "g_final"]


def kernel(**inputs):
    import numpy as np
    import concourse.bacc as bacc
    from concourse import mybir as mb
    from concourse.bass_utils import run_bass_kernel_spmd as run

    nc = bacc.Bacc("TRN2", target_bir_lowering=False, num_devices=1)
    arrays, args = {}, []
    for name in _INS:
        a = np.ascontiguousarray(inputs[name])
        arrays[f"in_{name}"] = a
        args.append(nc.dram_tensor(f"in_{name}", a.shape, mb.dt.from_np(a.dtype), kind="ExternalInput").ap())
    o = nc.dram_tensor("out_0", (1, SEQ, D), mb.dt.float32, kind="ExternalOutput").ap()
    build(nc, *args, o)
    r = run(nc, [arrays], core_ids=[0])
    return r.results[0]["out_0"]
```
